# Optimizing a Trainium2 kernel written in Bass

```python
import jax, jax.numpy as jnp
from jax import lax
import numpy as np

D_MODEL = 1024
BATCH = 1
SEQ = 512
DEPTH = 1

MEM_LEN = 256
MEM_HEADS = 4
MEM_HEAD_DIM = D_MODEL // 8
RET_HEADS = 4
RET_QK_DIM = D_MODEL // 8
RET_V_DIM = D_MODEL // 4
RET_CHUNK = 128
ROPE_BASE = 10000.0
POOL_WINDOWS = (2, 4, 8, 16)
POOL_GROUP = D_MODEL // 8
POOL_WIDTH = POOL_GROUP * len(POOL_WINDOWS)
FFN_HIDDEN = 4 * D_MODEL
N_BRANCHES = 3
EPS = 1e-6

RET_QK_W = RET_HEADS * RET_QK_DIM
RET_V_W = RET_HEADS * RET_V_DIM
MEM_Q_W = MEM_HEADS * MEM_HEAD_DIM
COL_SIZES = (RET_QK_W, RET_QK_W, RET_V_W, RET_V_W, POOL_WIDTH, MEM_Q_W, N_BRANCHES * D_MODEL)
COL_SPLITS = tuple(int(s) for s in np.cumsum(COL_SIZES)[:-1])
IN_PROJ_W = int(sum(COL_SIZES))

kernel_name = "hybrid_retention_pool_memory_encoder"

def rms_norm(x, g):
    xf = x.astype(jnp.float32)
    y = xf * lax.rsqrt(jnp.mean(jnp.square(xf), axis=-1, keepdims=True) + EPS)
    return (y * g.astype(jnp.float32)).astype(x.dtype)

def rotary(x, pos):
    d = x.shape[-1]
    inv = ROPE_BASE ** (-jnp.arange(0, d, 2, dtype=jnp.float32) / d)
    ang = pos.astype(jnp.float32)[:, None] * inv[None, :]
    cos = jnp.cos(ang)[None, :, None, :].astype(x.dtype)
    sin = jnp.sin(ang)[None, :, None, :].astype(x.dtype)
    x1, x2 = jnp.split(x, 2, axis=-1)
    return jnp.concatenate([x1 * cos - x2 * sin, x1 * sin + x2 * cos], axis=-1)

def retention_one_direction(q, k, v, log_g, strict):
    B, S, H, dk = q.shape
    dv = v.shape[-1]
    C = RET_CHUNK
    N = S // C
    q = q.reshape(B, N, C, H, dk)
    k = k.reshape(B, N, C, H, dk)
    v = v.reshape(B, N, C, H, dv)
    idx = jnp.arange(C, dtype=jnp.float32)
    diff = idx[:, None] - idx[None, :]
    mask = (diff > 0) if strict else (diff >= 0)
    dmat = jnp.where(mask[None], jnp.exp(log_g[:, None, None] * jnp.where(mask, diff, 0.0)[None]), 0.0)
    s = jnp.einsum('bnihd,bnjhd->bnhij', q, k) * dmat
    o_intra = jnp.einsum('bnhij,bnjhe->bnihe', s, v)
    zeta = jnp.exp(log_g[None, :] * (C - 1 - idx)[:, None])
    xi = jnp.exp(log_g[None, :] * (idx + 1)[:, None])
    chunk_decay = jnp.exp(log_g * C)
    qx = q * xi[:, :, None]
    kz = k * zeta[:, :, None]

    def step(state, inp):
        qc, kc, vc = inp
        out = jnp.einsum('bihd,bhde->bihe', qc, state)
        state = state * chunk_decay[None, :, None, None] + jnp.einsum('bjhd,bjhe->bhde', kc, vc)
        return state, out

    state0 = jnp.zeros((B, H, dk, dv), jnp.float32)
    _, o_cross = lax.scan(step, state0, (jnp.moveaxis(qx, 1, 0), jnp.moveaxis(kz, 1, 0), jnp.moveaxis(v, 1, 0)))
    o = o_intra.astype(jnp.float32) + jnp.moveaxis(o_cross, 0, 1)
    return o.reshape(B, S, H, dv)

def retention_branch(q, k, v, g, decay_logit, w_o, pos):
    B, S, _ = q.shape
    q = rotary(q.reshape(B, S, RET_HEADS, RET_QK_DIM), pos)
    k = rotary(k.reshape(B, S, RET_HEADS, RET_QK_DIM), pos) * (RET_QK_DIM ** -0.5)
    v = v.reshape(B, S, RET_HEADS, RET_V_DIM)
    log_g = jax.nn.log_sigmoid(decay_logit.astype(jnp.float32))
    o_fwd = retention_one_direction(q, k, v, log_g[0], strict=False)
    o_bwd = jnp.flip(retention_one_direction(jnp.flip(q, 1), jnp.flip(k, 1), jnp.flip(v, 1), log_g[1], strict=True), 1)
    o = o_fwd + o_bwd
    mu = jnp.mean(o, axis=-1, keepdims=True)
    var = jnp.mean(jnp.square(o - mu), axis=-1, keepdims=True)
    o = ((o - mu) * lax.rsqrt(var + EPS)).reshape(B, S, RET_V_W).astype(g.dtype)
    return (o * jax.nn.silu(g)) @ w_o

def pool_branch(p, w_grp, scale, w_o):
    B, S, _ = p.shape
    pf = p.astype(jnp.float32)
    cs = jnp.concatenate([jnp.zeros((B, 1, POOL_WIDTH), jnp.float32), jnp.cumsum(pf, axis=1)], axis=1)
    n = jnp.arange(S)
    groups = []
    for gi, w in enumerate(POOL_WINDOWS):
        lo = jnp.clip(n - w // 2, 0, S)
        hi = jnp.clip(n + w // 2, 0, S)
        sl = slice(gi * POOL_GROUP, (gi + 1) * POOL_GROUP)
        csg = cs[..., sl]
        mean = (csg[:, hi] - csg[:, lo]) / (hi - lo).astype(jnp.float32)[None, :, None]
        groups.append(mean - pf[..., sl])
    mixed = jnp.stack(groups, axis=2)
    y = jnp.einsum('bsgc,gcd->bsgd', mixed, w_grp.astype(jnp.float32)).reshape(B, S, POOL_WIDTH)
    y = (y * scale.astype(jnp.float32)).astype(p.dtype)
    return y @ w_o

def memory_branch(q, mem_n, w_kv, w_o):
    B, S, _ = q.shape
    M = mem_n.shape[1]
    q = q.reshape(B, S, MEM_HEADS, MEM_HEAD_DIM)
    kv = mem_n @ w_kv
    k, v = jnp.split(kv, 2, axis=-1)
    k = k.reshape(B, M, MEM_HEADS, MEM_HEAD_DIM)
    v = v.reshape(B, M, MEM_HEADS, MEM_HEAD_DIM)
    s = jnp.einsum('bshd,bmhd->bhsm', q, k).astype(jnp.float32) * (MEM_HEAD_DIM ** -0.5)
    a = jax.nn.softmax(s, axis=-1).astype(v.dtype)
    o = jnp.einsum('bhsm,bmhd->bshd', a, v).reshape(B, S, MEM_Q_W)
    return o @ w_o

def setup_inputs(seed: int = 0) -> dict:
    key = jax.random.key(seed)
    ks = jax.random.split(key, 20)
    f32 = jnp.float32

    def dense(k, shape, fan_in):
        return jax.random.normal(k, shape, f32) * (fan_in ** -0.5)

    base = 1.0 - 2.0 ** (-5.0 - jnp.arange(RET_HEADS, dtype=f32))
    base_logit = jnp.log(base) - jnp.log1p(-base)
    decay_logit = base_logit[None, None, :] + 0.05 * jax.random.normal(ks[3], (DEPTH, 2, RET_HEADS), f32)
    return {
        "x": jax.random.normal(ks[0], (BATCH, SEQ, D_MODEL), f32),
        "mem": jax.random.normal(ks[1], (BATCH, MEM_LEN, D_MODEL), f32),
        "w_in": dense(ks[2], (DEPTH, D_MODEL, IN_PROJ_W), D_MODEL),
        "ret_decay_logit": decay_logit,
        "w_ret_o": dense(ks[4], (DEPTH, RET_V_W, D_MODEL), RET_V_W),
        "w_pool_grp": dense(ks[5], (DEPTH, len(POOL_WINDOWS), POOL_GROUP, POOL_GROUP), POOL_GROUP),
        "pool_scale": 1.0 + 0.1 * jax.random.normal(ks[6], (DEPTH, POOL_WIDTH), f32),
        "w_pool_o": dense(ks[7], (DEPTH, POOL_WIDTH, D_MODEL), POOL_WIDTH),
        "w_mem_kv": dense(ks[8], (DEPTH, D_MODEL, 2 * MEM_Q_W), D_MODEL),
        "w_mem_o": dense(ks[9], (DEPTH, MEM_Q_W, D_MODEL), MEM_Q_W),
        "w_out": dense(ks[10], (DEPTH, D_MODEL, D_MODEL), D_MODEL),
        "w_ff1": dense(ks[11], (DEPTH, D_MODEL, FFN_HIDDEN), D_MODEL),
        "w_ff2": dense(ks[12], (DEPTH, FFN_HIDDEN, D_MODEL), FFN_HIDDEN),
        "norm1_g": 1.0 + 0.05 * jax.random.normal(ks[13], (DEPTH, D_MODEL), f32),
        "norm2_g": 1.0 + 0.05 * jax.random.normal(ks[14], (DEPTH, D_MODEL), f32),
        "mem_norm_g": 1.0 + 0.05 * jax.random.normal(ks[15], (D_MODEL,), f32),
        "final_norm_g": 1.0 + 0.05 * jax.random.normal(ks[16], (D_MODEL,), f32),
    }

def reference(x, mem, w_in, ret_decay_logit, w_ret_o, w_pool_grp, pool_scale, w_pool_o,
              w_mem_kv, w_mem_o, w_out, w_ff1, w_ff2, norm1_g, norm2_g, mem_norm_g, final_norm_g):
    S = x.shape[1]
    pos = jnp.arange(S)
    mem_n = rms_norm(mem, mem_norm_g)
    for l in range(DEPTH):
        h = rms_norm(x, norm1_g[l])
        proj = h @ w_in[l]
        q_r, k_r, v_r, g_r, p_in, q_m, gates = jnp.split(proj, COL_SPLITS, axis=-1)
        o_ret = retention_branch(q_r, k_r, v_r, g_r, ret_decay_logit[l], w_ret_o[l], pos)
        o_pool = pool_branch(p_in, w_pool_grp[l], pool_scale[l], w_pool_o[l])
        o_mem = memory_branch(q_m, mem_n, w_mem_kv[l], w_mem_o[l])
        gate_r, gate_p, gate_m = jnp.split(jax.nn.sigmoid(gates), N_BRANCHES, axis=-1)
        merged = (gate_r * o_ret + gate_p * o_pool + gate_m * o_mem).astype(x.dtype)
        x = x + merged @ w_out[l]
        h = rms_norm(x, norm2_g[l])
        x = x + jnp.square(jax.nn.relu(h @ w_ff1[l])) @ w_ff2[l]
    return rms_norm(x, final_norm_g)


_drawn_inputs = setup_inputs


def setup_inputs(seed=0):
    import zlib

    import numpy as np

    out = dict(_drawn_inputs(seed))
    spreads = {}
    factors = {'mem_norm_g': 8.0, 'pool_scale': 4.135, 'norm2_g': 3.112}
    for name, (base, spread) in spreads.items():
        noise = np.random.default_rng([zlib.crc32(name.encode()), seed]).standard_normal(out[name].shape)
        drawn = base * np.exp(spread * noise) if base else spread * noise
        out[name] = __import__('jax').numpy.asarray(drawn.astype(out[name].dtype))
    for name, factor in factors.items():
        out[name] = (out[name] * factor).astype(out[name].dtype)
    return out
```

```python
from contextlib import ExitStack

import numpy as np
import concourse.bass as bass
from concourse import mybir

FP32 = mybir.dt.float32
FP32R = mybir.dt.float32r
ALU = mybir.AluOpType
ACT = mybir.ActivationFunctionType
AX = mybir.AxisListType

P = 128
D = 1024
S = 512
KD = D // P
TT = S // P
M = 256
MT = M // P
HEADS = 4
VD = 256
POOL_WINDOWS = (2, 4, 8, 16)
PAD = max(POOL_WINDOWS) // 2
HIDDEN = 4 * D
N_BRANCHES = 3
EPS = 1e-6
QK_SCALE = float(P) ** -0.5
BLOCK = 1024
RING = 5
DEPTH = 4
AHEAD = 2
KB = 1024

COL_Q, COL_K, COL_V, COL_G = 0, 512, 1024, 2048
COL_POOL, COL_MQ, COL_GATES = 3072, 3584, 4096

REACH = S - P
SPAN = REACH + S


def projection_steps():
    order = [("turn", 0), ("turn", 1)]
    order += [("mem_k", h) for h in range(HEADS)]
    for b in range(4):
        order += [("mem_v", b), ("turn", MT + b)]
    order += [("mem_q", 0), ("mem_q", 1), ("att_s", 0), ("mem_q", 2), ("att_t", 0),
              ("mem_q", 3), ("att_o", 0),
              ("pool", 0), ("att_s", 1), ("pool", 1), ("mix", 0), ("att_t", 1),
              ("pool", 2), ("mix", 1), ("att_o", 1), ("pool", 3), ("mix", 2), ("att_s", 2)]
    more = {("q", 0): [("mix", 3), ("att_t", 2)], ("k", 0): [("att_o", 2)],
            ("v", 0): [("att_s", 3)], ("g", 0): [("att_t", 3)], ("g", 1): [("att_o", 3)]}
    for h in range(HEADS):
        for step in (("q", h), ("k", h), ("v", h), ("g", 2 * h), ("g", 2 * h + 1)):
            order += [step] + more.get(step, [])
            if step[0] == "q" and h > 0:
                order.append(("ret_t", h - 1))
            if step[0] == "v":
                order.append(("ret_s", 2 * h))
            if step == ("g", 2 * h):
                order.append(("ret_s", 2 * h + 1))
            if step == ("g", 2 * h + 1):
                order.append(("ret_v", h))
    order.append(("ret_t", HEADS - 1))

    fixed = {"mem_v": (4, 5), "v": (4, 5), "att_s": (6, 7), "att_t": (6, 7), "att_o": (2,),
             "ret_s": (2, 3), "ret_v": (6, 7), "ret_t": (6, 7)}
    blocks_of = {"turn": 0, "att_s": 0, "att_t": 0, "att_o": 0, "mix": 0, "ret_s": 0, "ret_v": 0,
                 "ret_t": 0, "v": 2}
    used = [0] * 8
    block, projected, steps = 0, 0, []
    for kind, i in order:
        if kind == "turn":
            banks = (6, 7) if i % 2 == 0 else (2, 3)
        elif kind in fixed:
            banks = fixed[kind]
        else:
            banks = (projected % 2,)
            projected += 1
        first = kind != "mem_v" or i == 0
        steps.append((kind, i, block, tuple((b, used[b] - (0 if first else 1)) for b in banks)))
        if first:
            for b in banks:
                used[b] += 1
        block += blocks_of.get(kind, 1)
    return steps, block, used


BLOCK_STEPS = ("mem_k", "mem_v", "mem_q", "pool", "q", "k", "v", "g")
LATE = 16 * 8


class Tally:

    def __init__(self):
        self.n = 0

    def next(self):
        self.n += 1
        return self.n


def slot_of(n, merge_first, merge_blocks):
    if merge_first <= n < merge_first + merge_blocks:
        return (n - merge_first) % 5
    return n % 4


def encoder_kernel(nc, x, mem, w_in, ret_decay_logit, w_ret_o, w_pool_grp, pool_scale, w_pool_o,
                   w_mem_kv, w_mem_o, w_out, w_ff1, w_ff2, norm1_g, norm2_g, mem_norm_g,
                   final_norm_g, identity, cos_table, sin_table, distance, inv_count, out):
    STEPS, MERGE0, USED_A = projection_steps()
    MERGE_BLOCKS = 5 * KD
    OUT0 = MERGE0 + MERGE_BLOCKS
    FFN0 = OUT0 + KD
    HALF = HIDDEN // P // 2
    GROUP = HALF // 2
    FFN_HALF_BLOCKS = HALF + 2 * GROUP
    BLOCKS = FFN0 + 2 * FFN_HALF_BLOCKS
    slots = [slot_of(n, MERGE0, MERGE_BLOCKS) for n in range(BLOCKS)]
    loads = [slots[:n + 1].count(slots[n]) for n in range(BLOCKS)]
    FF1_BANKS = ((0, 1), (2, 3))
    FF2_BANKS = (((2, 3, 4, 5), (6, 7, 0, 1)), ((4, 5, 6, 7), (0, 1, 2, 3)))

    used_merge = list(USED_A)
    used_out = [u + (KD if b < 6 else 0) for b, u in enumerate(used_merge)]
    used_ffn = list(used_out)
    for b, n in ((0, KD // 2), (1, KD // 2), (2, 1), (6, KD), (7, KD)):
        used_ffn[b] += n

    ff1_uses, ffn_uses, at_now = [], [], list(used_ffn)
    for half in range(2):
        ff1_uses.append([at_now[b] for b in FF1_BANKS[half]])
        for b in FF1_BANKS[half]:
            at_now[b] += HALF // 2
        ffn_uses.append([])
        for f in range(2):
            ffn_uses[half].append([at_now[b] for b in FF2_BANKS[half][f]])
            for b in FF2_BANKS[half][f]:
                at_now[b] += 1
    pool_block = {}
    for kind, i, n, _ in STEPS:
        if kind == "pool":
            pool_block[i] = n

    ctx = ExitStack()
    with ctx:
        BASE = 16512

        def at(name, kb, shape, dtype=FP32):
            size = int(np.prod(shape[1:])) * 4
            assert BASE + kb * KB + size <= 229344, name
            return nc.alloc_sbuf_tensor_at(name, shape, dtype, offset=int(BASE + kb * KB))

        def sem(name):
            return ctx.enter_context(nc.semaphore(name))

        h_hi, h_lo = at("h_hi", 0, [P, KD, S], FP32R), at("h_lo", 16, [P, KD, S], FP32R)
        w_hi = [at(f"w_hi{s}", 32 + 4 * s, [P, BLOCK], FP32R) for s in range(RING)]
        w_lo = [at(f"w_lo{s}", 52 + 4 * s, [P, BLOCK], FP32R) for s in range(RING)]
        w_raw = [at(f"w_raw{s}", 72 + 4 * s, [P, BLOCK]) for s in range(RING)]
        swapped, work_a = at("swapped", 48, [P, S]), at("work_a", 50, [P, S])
        work_b, sig_g = at("work_b", 68, [P, S]), at("sig_g", 70, [P, S])
        square_junk, o_nat = at("square_junk", 88, [P, D]), at("o_nat", 88, [P, TT, VD])
        memT_hi, memT_lo = at("memT_hi", 92, [P, KD, M], FP32R), at("memT_lo", 108, [P, KD, M], FP32R)
        memK_hi, memK_lo = at("memK_hi", 100, [P, HEADS, M], FP32R), at("memK_lo", 116, [P, HEADS, M], FP32R)
        memV_hi, memV_lo = at("memV_hi", 104, [P, MT, S], FP32R), at("memV_lo", 120, [P, MT, S], FP32R)
        probT_hi, probT_lo = at("probT_hi", 92, [P, MT, S], FP32R), at("probT_lo", 108, [P, MT, S], FP32R)
        probs = at("probs", 96, [P, TT, M])
        ret_hi, ret_lo = at("ret_hi", 92, [P, KD, S], FP32R), at("ret_lo", 108, [P, KD, S], FP32R)
        mq_hi, mq_lo = at("mq_hi", 124, [P, HEADS, S], FP32R), at("mq_lo", 132, [P, HEADS, S], FP32R)
        att_hi, att_lo = at("att_hi", 124, [P, HEADS, S], FP32R), at("att_lo", 132, [P, HEADS, S], FP32R)
        pool_hi, pool_lo = at("pool_hi", 140, [P, 4, S], FP32R), at("pool_lo", 148, [P, 4, S], FP32R)
        stage = [at(f"stage{s}", 156 + 4 * s, [P, D]) for s in range(MT + TT)]
        grp_raw = at("grp_raw", 68, [P, 4, P])
        grp_hi, grp_lo = at("grp_hi", 70, [P, 4, P], FP32R), at("grp_lo", 205, [P, 4, P], FP32R)
        mix_hi, mix_lo = at("mix_hi", 168, [P, S], FP32R), at("mix_lo", 170, [P, S], FP32R)
        padded = [at(f"padded{s}", 172 + 2.125 * s, [P, S + 2 * PAD]) for s in range(3)]
        counts = at("counts", 180, [P, 4, S])
        qk_hi, qk_lo = at("qk_hi", 156, [P, 2, S], FP32R), at("qk_lo", 160, [P, 2, S], FP32R)
        v_hi, v_lo = at("v_hi", 164, [P, TT, VD], FP32R), at("v_lo", 168, [P, TT, VD], FP32R)
        s_hi, s_lo = at("s_hi", 172, [P, TT, S], FP32R), at("s_lo", 180, [P, TT, S], FP32R)
        decay_a, decay_b = at("decay_a", 172, [P, SPAN]), at("decay_b", 176, [P, SPAN])
        mrg_hi, mrg_lo = at("mrg_hi", 156, [P, KD, S], FP32R), at("mrg_lo", 172, [P, KD, S], FP32R)
        ident = at("ident", 188, [P, P])
        cos, sin = at("cos", 189, [P, S]), at("sin", 191, [P, S])
        dist, decay = at("dist", 193, [P, SPAN]), at("decay", 197, [P, SPAN])
        gate_g, work_c = at("gate_g", 201, [P, 2, S]), at("work_c", 205, [P, S])
        gain_x, gain_mem = at("gain_x", 197, [P, D]), at("gain_mem", 201, [P, D])
        sig = [at("sig_ret", 189, [P, S]), at("sig_pool", 191, [P, S]), at("sig_mem", 193, [P, S])]
        x_cols = [at(f"x_cols{s}", 197 + 2 * s, [P, TT, P]) for s in range(4)]
        sumsq, square = at("sumsq", 205, [P, S]), [at("square0", 2, [P, S]), at("square1", 4, [P, S])]
        h2_hi, h2_lo = at("h2_hi", 92, [P, KD, S], FP32R), at("h2_lo", 108, [P, KD, S], FP32R)
        x1T, x1 = at("x1T", 124, [P, KD, S]), at("x1", 140, [P, TT, D])
        hid_hi, hid_lo = at("hid_hi", 0, [P, HALF, S], FP32R), at("hid_lo", 156, [P, HALF, S], FP32R)
        relu = [at("relu0", 189, [P, S]), at("relu1", 191, [P, S])]
        relu2 = [at("relu2_0", 193, [P, S]), at("relu2_1", 195, [P, S])]
        gain_f = at("gain_f", 197, [P, D])
        y = [at(f"y{t}", 92 + 4 * t, [P, D]) for t in range(TT)]

        taken = [0]

        def tiny(name, n):
            taken[0] += n
            assert taken[0] <= 192
            return at(name, 207 + (taken[0] - n) * 4 / KB, [P, n])

        ssq, msq, rms = tiny("ssq", 8), tiny("msq", 8), tiny("rms", 8)
        minus_half, mean_col = tiny("minus_half", 8), tiny("mean_col", 8)
        logit, lg_work, exp_abs = tiny("logit", 8), tiny("lg_work", 8), tiny("exp_abs", 8)
        lg_z, lg_z2, log_g = tiny("lg_z", 8), tiny("lg_z2", 8), tiny("log_g", 8)
        pscale, gain2 = tiny("pscale", 8), tiny("gain2", 8)
        row_max, row_sum, row_inv = tiny("row_max", 8), tiny("row_sum", 8), tiny("row_inv", 8)
        ret_var, ret_rstd = tiny("ret_var", 8), tiny("ret_rstd", 8)
        stats, moments = tiny("stats", 24), tiny("moments", 8)
        inv_ms = tiny("inv_ms", 8)

        bank = [ctx.enter_context(nc.psum_tensor(f"bank{b}", [P, S], FP32)) for b in range(8)]

        stage_in = [sem(f"stage_in{s}") for s in range(MT + TT)]
        early_in, late_in, gain_in = sem("early_in"), sem("late_in"), sem("gain_in")
        grp_rounded, grp_split, mix_done = sem("grp_rounded"), sem("grp_split"), sem("mix_done")
        raw_in = [sem(f"raw_in{s}") for s in range(RING)]
        x_cols_in = [sem(f"x_cols_in{s}") for s in range(4)]
        stored, slots_cleared = sem("stored"), sem("slots_cleared")
        hi_split, lo_split = sem("hi_split"), sem("lo_split")
        blocks_done = sem("blocks_done")
        bank_free = [sem(f"bank_free{b}") for b in range(8)]
        hi_written = sem("hi_written")
        to_round = sem("to_round")
        consts_set = sem("consts_set")
        squares_summed, msq_set, rms_set = sem("squares_summed"), sem("msq_set"), sem("rms_set")
        normed = sem("normed")
        turned = sem("turned")
        scores_done, probs_turned, att_done = sem("scores_done"), sem("probs_turned"), sem("att_done")
        max_set, probs_set = sem("max_set"), sem("probs_set")
        logit_abs, logit_exp = sem("logit_abs"), sem("logit_exp")
        mixed, pads_set = sem("mixed"), sem("pads_set")
        halves_swapped, sin_done = sem("halves_swapped"), sem("sin_done")
        qk_ready = sem("qk_ready")
        log_decay_set, decay_set = sem("log_decay_set"), sem("decay_set")
        ret_scores_done, s_ready, ret_values_done = sem("ret_scores_done"), sem("s_ready"), sem("ret_values_done")
        var_set, rstd_set = sem("var_set"), sem("rstd_set")
        ret_turned, ret_ready = sem("ret_turned"), sem("ret_ready")
        sigmoid_g = sem("sigmoid_g")
        merged_ready = sem("merged_ready")
        x_turned, x1_turned, square_set, sumsq_set = sem("x_turned"), sem("x1_turned"), sem("square_set"), sem("sumsq_set")
        h2_ready, hid_ready = sem("h2_ready"), sem("hid_ready")
        ms_done = sem("ms_done")
        half_sums, y_ready = sem("half_sums"), sem("y_ready")
        vec_step, pool_step = sem("vec_step"), sem("pool_step")

        banks_of = {(kind, i): banks for kind, i, _, banks in STEPS}

        w_in_v = w_in.rearrange("l (k p) n -> (l p) k n", p=P)
        kv_v = w_mem_kv.rearrange("l (k p) n -> (l p) k n", p=P)
        ret_o_v = w_ret_o.rearrange("l (k p) n -> (l p) k n", p=P)
        pool_o_v = w_pool_o.rearrange("l (k p) n -> (l p) k n", p=P)
        mem_o_v = w_mem_o.rearrange("l (k p) n -> (l p) k n", p=P)
        out_v = w_out.rearrange("l (k p) n -> (l p) k n", p=P)
        ff1_v = w_ff1.rearrange("l (k p) n -> (l p) k n", p=P)
        ff2_v = w_ff2.rearrange("l (k p) n -> (l p) k n", p=P)
        x_v = x.rearrange("b (t p) d -> (b p) t d", p=P)
        mem_v = mem.rearrange("b (t p) d -> (b p) t d", p=P)
        y_v = out.rearrange("b (t p) d -> (b p) t d", p=P)

        def r32(ap):
            return ap.bitcast(FP32)

        block = ctx.enter_context(nc.Block())

        @block.sync
        def _(sp):
            def load(n, view, k0, k1, col, width, turn=0):
                if n >= DEPTH:
                    sp.wait_ge(lo_split, turn + n - DEPTH + 1)
                    if not isinstance(turn, int):
                        sp.sem_inc(slots_cleared, 1)
                sp.dma_start(w_raw[slots[n]][:, :].rearrange("p (k n) -> p k n", n=width),
                             view[:, k0:k1, bass.ds(col, width)]).then_inc(raw_in[slots[n]], 16)

            for kind, i, n, _ in STEPS:
                if kind == "mem_k":
                    load(n, kv_v, 0, KD, i * P, P)
                elif kind == "mem_v":
                    load(n, kv_v, 2 * i, 2 * i + 2, HEADS * P, S)
                elif kind == "v":
                    load(n, w_in_v, 0, 4, COL_V + i * VD, VD)
                    load(n + 1, w_in_v, 4, KD, COL_V + i * VD, VD)
                elif kind in ("mem_q", "pool", "q", "k", "g"):
                    col = {"mem_q": COL_MQ, "pool": COL_POOL, "q": COL_Q, "k": COL_K, "g": COL_G}[kind]
                    load(n, w_in_v, 0, KD, col + i * P, P)

            def load_gates(m, shift, turn):
                for b in range(N_BRANCHES):
                    load(MERGE0 + 5 * shift + b, w_in_v, 0, KD, COL_GATES + b * D + m * P, P, turn)
                load(MERGE0 + 5 * shift + 3, ret_o_v, 0, KD, m * P, P, turn)

            def load_pool_mem(m, turn):
                n = MERGE0 + 4
                sp.wait_ge(lo_split, turn + n - DEPTH + 1)
                if not isinstance(turn, int):
                    sp.sem_inc(slots_cleared, 1)
                raw = w_raw[slots[n]]
                sp.dma_start(raw[:, 0:S].rearrange("p (k n) -> p k n", n=P),
                             pool_o_v[:, :, bass.ds(m * P, P)]).then_inc(raw_in[slots[n]], 16)
                sp.dma_start(raw[:, S:BLOCK].rearrange("p (k n) -> p k n", n=P),
                             mem_o_v[:, :, bass.ds(m * P, P)]).then_inc(raw_in[slots[n]], 16)

            load_gates(0, 0, 0)
            sp.wait_ge(ret_ready, KD)
            with sp.Fori(0, KD - 1) as m:
                load_pool_mem(m, 5 * m)
                load_gates(m + 1, 1, 5 * m)
            load_pool_mem(KD - 1, 5 * (KD - 1))

            for s in range(4):
                sp.dma_start(x_cols[s][:, :, :], x_v[:, :, s * P:(s + 1) * P]).then_inc(x_cols_in[s], 16)
            for m in range(KD):
                load(OUT0 + m, out_v, 0, KD, m * P, P)
                if m >= 4:
                    sp.wait_ge(x_turned, m - 3)
                    sp.dma_start(x_cols[m - 4][:, :, :], x_v[:, :, m * P:(m + 1) * P]).then_inc(x_cols_in[m - 4], 16)

            for half in range(2):
                n0 = FFN0 + half * FFN_HALF_BLOCKS
                with sp.Fori(0, HALF // 4) as q:
                    for jj in range(4):
                        load(n0 + jj, ff1_v, 0, KD, q * (4 * P) + (half * HALF + jj) * P, P, 4 * q)
                if half == 0:
                    sp.wait_ge(x_turned, KD)
                    sp.dma_start(gain_f[:, :], final_norm_g.rearrange("(a n) -> a n", a=1).broadcast_to([P, D]))\
                        .then_inc(gain_in, 16)
                for f in range(2):
                    for b in range(GROUP):
                        k = half * HALF + 2 * b
                        load(n0 + HALF + f * GROUP + b, ff2_v, k, k + 2, f * S, S)

            for t in range(TT):
                sp.wait_ge(y_ready, t + 1)
                sp.dma_start(y_v[:, t, :], y[t][:, :]).then_inc(stored, 16)
            sp.wait_ge(stored, 16 * TT)

        @block.tensor
        def _(pe):
            def three(out_ap, wh, wl, xh, xl, first, last):
                pe.matmul(out_ap, wh, xh, start=first, stop=False)
                pe.matmul(out_ap, wh, xl, start=False, stop=False)
                return pe.matmul(out_ap, wl, xh, start=False, stop=last)

            def project(s, out_ap, x_hi, x_lo, tiles, w0=0):
                for k in range(tiles):
                    c = slice((w0 + k) * P, (w0 + k + 1) * P)
                    last = three(out_ap, w_hi[s][:, c], w_lo[s][:, c], x_hi[:, k, :], x_lo[:, k, :],
                                 k == 0, k == tiles - 1)
                return last

            def free(b, uses):
                if uses:
                    pe.wait_ge(bank_free[b], uses)

            def read_out(kind, i):
                for b, uses in banks_of[kind, i]:
                    pe.wait_ge(bank_free[b], uses + 1)

            pe.wait_ge(early_in, 48)
            for kind, i, n, banks in STEPS:
                for b, uses in banks:
                    if kind != "mem_v" or i == 0:
                        free(b, uses)
                if kind == "turn":
                    pe.wait_ge(normed, i + 1)
                    for c, (b, _) in enumerate(banks):
                        for k in range(4):
                            f = (4 * c + k) * P
                            last = pe.transpose(bank[b][:, k * P:(k + 1) * P], stage[i][:, f:f + P], ident[:, :])
                        last.then_inc(turned, 1)
                elif kind == "mem_k":
                    pe.wait_ge(lo_split, n + 1)
                    if i == 0:
                        for t in range(MT):
                            read_out("turn", t)
                    project(slots[n], bank[banks[0][0]][:, 0:M], memT_hi, memT_lo, KD).then_inc(blocks_done, 1)
                elif kind == "mem_v":
                    pe.wait_ge(lo_split, n + 1)
                    for t in range(MT):
                        for kk in range(2):
                            k = 2 * i + kk
                            c = slice(kk * S, (kk + 1) * S)
                            tok = slice(t * P, (t + 1) * P)
                            last = three(bank[banks[t][0]][:, :], memT_hi[:, k, tok], memT_lo[:, k, tok],
                                         w_hi[slots[n]][:, c], w_lo[slots[n]][:, c], k == 0, k == KD - 1)
                    last.then_inc(blocks_done, 1)
                elif kind in ("mem_q", "pool", "q", "k", "g"):
                    pe.wait_ge(lo_split, n + 1)
                    if kind == "mem_q" and i == 0:
                        for t in range(MT, MT + TT):
                            read_out("turn", t)
                    project(slots[n], bank[banks[0][0]][:, :], h_hi, h_lo, KD).then_inc(blocks_done, 1)
                elif kind == "v":
                    pe.wait_ge(lo_split, n + 2)
                    for t in range(TT):
                        tok = slice(t * P, (t + 1) * P)
                        dst = bank[banks[t // 2][0]][:, (t % 2) * VD:(t % 2 + 1) * VD]
                        for k in range(KD):
                            s, c = slots[n + k // 4], slice((k % 4) * VD, (k % 4 + 1) * VD)
                            last = three(dst, h_hi[:, k, tok], h_lo[:, k, tok], w_hi[s][:, c], w_lo[s][:, c],
                                         k == 0, k == KD - 1)
                            if t == TT - 1 and k == KD - 2:
                                last.then_inc(blocks_done, 1)
                    last.then_inc(blocks_done, 1)
                elif kind == "mix":
                    pe.wait_ge(mixed, i + 1)
                    pe.wait_ge(grp_split, 1)
                    b = banks[0][0]
                    three(bank[b][:, :], grp_hi[:, i, :], grp_lo[:, i, :], mix_hi[:, :], mix_lo[:, :],
                          True, True).then_inc(mix_done, 1)
                elif kind == "att_s":
                    read_out("mem_q", i)
                    for t in range(TT):
                        tok = slice(t * P, (t + 1) * P)
                        last = three(bank[banks[t // 2][0]][:, (t % 2) * M:(t % 2 + 1) * M],
                                     mq_hi[:, i, tok], mq_lo[:, i, tok], memK_hi[:, i, :], memK_lo[:, i, :],
                                     True, True)
                    last.then_inc(scores_done, 1)
                elif kind == "att_t":
                    pe.wait_ge(probs_set, i + 1)
                    for c in range(MT):
                        for t in range(TT):
                            last = pe.transpose(bank[banks[c][0]][:, t * P:(t + 1) * P],
                                                probs[:, t, c * P:(c + 1) * P], ident[:, :])
                    last.then_inc(probs_turned, 1)
                elif kind == "att_o":
                    if i == 0:
                        read_out("mem_v", 0)
                    read_out("att_t", i)
                    for c in range(MT):
                        d = slice(i * P, (i + 1) * P)
                        last = three(bank[banks[0][0]][:, :], memV_hi[:, c, d], memV_lo[:, c, d],
                                     probT_hi[:, c, :], probT_lo[:, c, :], c == 0, c == MT - 1)
                    last.then_inc(att_done, 1)
                elif kind == "ret_s":
                    hd, p = i // 2, i % 2
                    pe.wait_ge(qk_ready, 2 * hd + 2)
                    for jj in range(2):
                        j = 2 * p + jj
                        last = three(bank[banks[jj][0]][:, :], qk_hi[:, 1, j * P:(j + 1) * P],
                                     qk_lo[:, 1, j * P:(j + 1) * P], qk_hi[:, 0, :], qk_lo[:, 0, :], True, True)
                        last.then_inc(ret_scores_done, 1)
                elif kind == "ret_v":
                    pe.wait_ge(s_ready, 4 * i + 4)
                    read_out("v", i)
                    for t in range(TT):
                        tok = slice(t * P, (t + 1) * P)
                        for j in range(TT):
                            last = three(bank[banks[t // 2][0]][:, (t % 2) * VD:(t % 2 + 1) * VD],
                                         s_hi[:, j, tok], s_lo[:, j, tok], v_hi[:, j, :], v_lo[:, j, :],
                                         j == 0, j == TT - 1)
                    last.then_inc(ret_values_done, 1)
                elif kind == "ret_t":
                    read_out("ret_v", i)
                    for c in range(2):
                        for t in range(TT):
                            last = pe.transpose(bank[banks[c][0]][:, t * P:(t + 1) * P],
                                                o_nat[:, t, c * P:(c + 1) * P], ident[:, :])
                        last.then_inc(ret_turned, 1)

            for i in range(4):
                read_out("mix", i)
                read_out("att_o", i)
            with pe.Fori(0, KD) as m:
                for g in range(N_BRANCHES):
                    pe.wait_ge(lo_split, 5 * m + MERGE0 + g + 1)
                    pe.wait_ge(bank_free[g], m + used_merge[g])
                    project(g, bank[g][:, :], h_hi, h_lo, KD).then_inc(blocks_done, 1)
                pe.wait_ge(lo_split, 5 * m + MERGE0 + 4)
                pe.wait_ge(bank_free[3], m + used_merge[3])
                pe.wait_ge(ret_ready, KD)
                project(3, bank[3][:, :], ret_hi, ret_lo, KD).then_inc(blocks_done, 1)
                pe.wait_ge(lo_split, 5 * m + MERGE0 + 5)
                pe.wait_ge(bank_free[4], m + used_merge[4])
                project(4, bank[4][:, :], pool_hi, pool_lo, 4)
                pe.wait_ge(bank_free[5], m + used_merge[5])
                project(4, bank[5][:, :], att_hi, att_lo, 4, 4).then_inc(blocks_done, 1)

            def turn_back(m):
                pe.wait_ge(bank_free[m % 2], used_out[m % 2] + m // 2 + 1)
                free(7, used_out[7] + m)
                for t in range(TT):
                    last = pe.transpose(bank[7][:, t * P:(t + 1) * P], x1T[:, m, t * P:(t + 1) * P], ident[:, :])
                last.then_inc(x1_turned, 1)

            for m in range(KD):
                pe.wait_ge(x_cols_in[m % 4], 16 * (m // 4 + 1))
                free(6, used_out[6] + m)
                for t in range(TT):
                    last = pe.transpose(bank[6][:, t * P:(t + 1) * P], x_cols[m % 4][:, t, :], ident[:, :])
                last.then_inc(x_turned, 1)
                if m == 0:
                    pe.wait_ge(merged_ready, KD + 1)
                pe.wait_ge(lo_split, OUT0 + m + 1)
                free(m % 2, used_out[m % 2] + m // 2)
                project(slots[OUT0 + m], bank[m % 2][:, :], mrg_hi, mrg_lo, KD).then_inc(blocks_done, 1)
                if m:
                    turn_back(m - 1)
            turn_back(KD - 1)

            uses = list(used_ffn)
            pe.wait_ge(h2_ready, KD)
            for half in range(2):
                n0 = FFN0 + half * FFN_HALF_BLOCKS
                pair = FF1_BANKS[half]
                with pe.Fori(0, HALF // 4) as q:
                    for jj in range(4):
                        b = pair[jj % 2]
                        pe.wait_ge(lo_split, 4 * q + n0 + jj + 1)
                        pe.wait_ge(bank_free[b], 2 * q + uses[b] + jj // 2)
                        project(slots[n0 + jj], bank[b][:, :], h2_hi, h2_lo, KD).then_inc(blocks_done, 1)
                for b in pair:
                    uses[b] += HALF // 2
                if half == 0:
                    pe.wait_ge(sumsq_set, KD - 1)
                    free(2, used_out[2])
                    for t in range(TT):
                        last = pe.matmul(bank[2][:, t:t + 1], sumsq[:, t * P:(t + 1) * P], mean_col[:, 0:1],
                                         start=True, stop=True)
                    last.then_inc(ms_done, 1)
                for f in range(2):
                    four = FF2_BANKS[half][f]
                    for b in four:
                        free(b, uses[b])
                        uses[b] += 1
                    for g in range(GROUP):
                        n = n0 + HALF + f * GROUP + g
                        pe.wait_ge(lo_split, n + 1)
                        pe.wait_ge(hid_ready, half * HALF + 2 * g + 2)
                        for t in range(TT):
                            tok = slice(t * P, (t + 1) * P)
                            for kk in range(2):
                                k, c = 2 * g + kk, slice(kk * S, (kk + 1) * S)
                                last = three(bank[four[t]][:, :], hid_hi[:, k, tok], hid_lo[:, k, tok],
                                             w_hi[slots[n]][:, c], w_lo[slots[n]][:, c],
                                             k == 0, k == HALF - 1)
                        last.then_inc(blocks_done, 1)

        @block.scalar
        def _(act):
            for s in range(MT + TT):
                src = mem_v[:, s, :] if s < MT else x_v[:, s - MT, :]
                act.dma_start(stage[s][:, :], src).then_inc(stage_in[s], 16)
                if s == 0:
                    act.dma_start(ident[:, :], identity).then_inc(early_in, 16)
                    act.dma_start(gain_mem[:, :], mem_norm_g.rearrange("(a n) -> a n", a=1).broadcast_to([P, D])).then_inc(early_in, 16)
                if s == 2:
                    act.dma_start(gain_x[:, :], norm1_g.broadcast_to([P, D])).then_inc(early_in, 16)
            act.dma_start(pscale[:, 0:4], pool_scale.rearrange("l (g c) -> c (l g)", c=P),
                          allow_slow_non_contiguous=True).then_inc(late_in, 16)
            act.dma_start(gain2[:, :], norm2_g.rearrange("l (k c) -> c (l k)", c=P),
                          allow_slow_non_contiguous=True).then_inc(late_in, 16)
            act.dma_start(logit[:, :], ret_decay_logit.rearrange("l a h -> l (a h)").broadcast_to([P, 8]))\
                .then_inc(late_in, 16)
            act.dma_start(grp_raw[:, :, :], w_pool_grp.rearrange("l g c d -> (l c) g d")).then_inc(late_in, 16)
            act.dma_start(cos[:, :], cos_table).then_inc(late_in, 16)
            act.dma_start(sin[:, :], sin_table).then_inc(late_in, 16)
            act.dma_start(dist[:, :], distance).then_inc(late_in, 16)
            act.dma_start(counts[:, :, :].rearrange("p g s -> p (g s)"), inv_count.broadcast_to([P, 4 * S]))\
                .then_inc(late_in, 16)

            rounds = Tally()

            def split(n, per=0, i=0):
                s = slots[n]
                act.wait_ge(raw_in[s], 32 * i + 32 if s == RING - 1 else 16 * i + 16 * loads[n])
                if n >= DEPTH:
                    act.wait_ge(blocks_done, per * i + n - DEPTH + 1)
                act.activation(w_hi[s][:, :], w_raw[s][:, :], ACT.Copy).then_inc(hi_split, 1)

            def round_to(dst, src, scale=1.0):
                act.activation(dst, src, ACT.Copy, scale=scale).then_inc(hi_written, 1)

            def square_rows(s):
                act.wait_ge(stage_in[s], 16)
                if s:
                    act.wait_ge(squares_summed, s)
                act.activation(square_junk[:, :], stage[s][:, :], ACT.Square,
                               accum_out=ssq[:, s:s + 1]).then_inc(squares_summed, 1)

            square_rows(0)
            square_rows(1)
            for kind, i, n, banks in STEPS:
                b = banks[0][0]
                if (kind, i) == ("mem_k", 0):
                    for first in range(AHEAD):
                        split(first)
                if kind in BLOCK_STEPS:
                    for more in range(2 if kind == "v" else 1):
                        split(n + AHEAD + more)
                if kind == "turn":
                    hi = memT_hi if i < MT else h_hi
                    tok = slice((i % MT) * P, (i % MT + 1) * P) if i < MT else slice((i - MT) * P, (i - MT + 1) * P)
                    for c, (b, _) in enumerate(banks):
                        act.wait_ge(turned, 2 * i + c + 1)
                        round_to(hi[:, 4 * c:4 * c + 4, tok], bank[b][:, :].rearrange("p (k n) -> p k n", n=P))
                elif kind == "mem_k":
                    act.wait_ge(blocks_done, n + 1)
                    round_to(memK_hi[:, i, :], bank[b][:, 0:M])
                    square_rows(MT + i)
                elif kind == "mem_v" and i == 3:
                    act.wait_ge(blocks_done, n + 1)
                    for t in range(MT):
                        round_to(memV_hi[:, t, :], bank[banks[t][0]][:, :])
                elif kind == "mem_q":
                    if i == 0:
                        act.wait_ge(logit_abs, 1)
                        act.activation(exp_abs[:, :], lg_work[:, :], ACT.Exp).then_inc(logit_exp, 1)
                        act.activation(grp_hi[:, :, :], grp_raw[:, :, :], ACT.Copy).then_inc(grp_rounded, 1)
                    act.wait_ge(blocks_done, n + 1)
                    round_to(mq_hi[:, i, :], bank[b][:, :])
                elif kind == "pool":
                    act.wait_ge(to_round, rounds.next())
                    if i:
                        act.wait_ge(mix_done, i)
                    round_to(mix_hi[:, :], work_a[:, :])
                elif kind == "mix":
                    act.wait_ge(mix_done, i + 1)
                    round_to(pool_hi[:, i, :], bank[b][:, :], pscale[:, i:i + 1])
                elif kind == "att_s":
                    act.wait_ge(max_set, i + 1)
                    for t in range(TT):
                        e = act.activation(probs[:, t, :], bank[banks[t // 2][0]][:, (t % 2) * M:(t % 2 + 1) * M],
                                           ACT.Exp, bias=row_max[:, t:t + 1], scale=QK_SCALE,
                                           accum_out=row_sum[:, t:t + 1])
                        if t % 2:
                            e.then_inc(bank_free[banks[t // 2][0]], 1)
                elif kind == "att_t":
                    act.wait_ge(probs_turned, i + 1)
                    for c in range(MT):
                        round_to(probT_hi[:, c, :], bank[banks[c][0]][:, :])
                elif kind == "att_o":
                    act.wait_ge(att_done, i + 1)
                    round_to(att_hi[:, i, :], bank[b][:, :])
                elif kind in ("q", "k"):
                    act.wait_ge(blocks_done, n + 1)
                    turn = 2 * i + (kind == "k")
                    if turn:
                        act.wait_ge(sin_done, turn)
                    half = P // 2
                    act.activation(swapped[0:half, :], bank[b][half:P, :], ACT.Copy)
                    act.activation(swapped[half:P, :], bank[b][0:half, :], ACT.Copy).then_inc(halves_swapped, 1)
                    act.wait_ge(to_round, rounds.next())
                    round_to(qk_hi[:, int(kind == "k"), :], work_a[:, :])
                    if kind == "k":
                        act.wait_ge(log_decay_set, i + 1)
                        act.activation(decay[:, :], decay_a[:, :], ACT.Exp).then_inc(decay_set, 1)
                elif kind == "v":
                    act.wait_ge(blocks_done, n + 2)
                    for c, (b, _) in enumerate(banks):
                        round_to(v_hi[:, 2 * c:2 * c + 2, :], bank[b][:, :].rearrange("p (t e) -> p t e", e=VD))
                elif kind == "g":
                    act.wait_ge(blocks_done, n + 1)
                    if i:
                        b0, uses = banks_of["g", i - 1][0]
                        act.wait_ge(bank_free[b0], uses + 1)
                    act.activation(sig_g[:, :], bank[b][:, :], ACT.Sigmoid).then_inc(sigmoid_g, 1)
                elif kind == "ret_s":
                    for jj, (b, uses) in enumerate(banks):
                        act.wait_ge(bank_free[b], uses + 1)
                        round_to(s_hi[:, 2 * (i % 2) + jj, :], (work_a, work_c)[jj][:, :])
                elif kind == "ret_t":
                    for c, (b, uses) in enumerate(banks):
                        act.wait_ge(bank_free[b], uses + 1)
                        round_to(ret_hi[:, 2 * i + c, :], (work_a, work_c)[c][:, :])

            act.preload_act_table(ACT.Sigmoid)
            with act.Fori(0, KD) as m:
                for g in range(N_BRANCHES):
                    split(MERGE0 + AHEAD + g, 5, m)
                    act.wait_ge(blocks_done, 5 * m + MERGE0 + g + 1)
                    if g == 0:
                        act.wait_ge(merged_ready, m + 1)
                    act.activation(sig[g][:, :], bank[g][:, :], ACT.Sigmoid).then_inc(bank_free[g], 1)
                split(MERGE0 + AHEAD + 3, 5, m)
                split(MERGE0 + AHEAD + 4, 5, m)
                act.wait_ge(to_round, m + rounds.n + 1)
                round_to(mrg_hi[:, bass.ds(m, 1), :], sig[0][:, :].rearrange("p (a s) -> p a s", a=1))
            rounds.n += KD

            act.wait_ge(blocks_done, OUT0)

            def back(m):
                act.wait_ge(x1_turned, m + 1)
                act.activation(x1[:, :, m * P:(m + 1) * P], bank[7][:, :].rearrange("p (t n) -> p t n", n=P),
                               ACT.Copy).then_inc(bank_free[7], 1)

            for m in range(KD):
                split(OUT0 + m + AHEAD)
                act.wait_ge(x_turned, m + 1)
                act.activation(x1T[:, m, :], bank[6][:, :], ACT.Copy).then_inc(bank_free[6], 1)
                if m:
                    back(m - 1)
                act.wait_ge(bank_free[m % 2], used_out[m % 2] + m // 2 + 1)
                if m >= 3:
                    act.wait_ge(sumsq_set, m - 2)
                act.activation((square[m % 2] if m else sumsq)[:, :], x1T[:, m, :], ACT.Square).then_inc(square_set, 1)
                round_to(h2_hi[:, m, :], x1T[:, m, :], gain2[:, m:m + 1])
            back(KD - 1)

            act.wait_ge(sumsq_set, KD - 1)
            for half in range(2):
                n0 = FFN0 + half * FFN_HALF_BLOCKS
                pair = FF1_BANKS[half]
                with act.Fori(0, HALF // 4) as q:
                    for jj in range(4):
                        b = pair[jj % 2]
                        split(n0 + jj + AHEAD, 4, q)
                        act.wait_ge(blocks_done, 4 * q + n0 + jj + 1)
                        act.activation(relu[jj % 2][:, :], bank[b][:, :], ACT.Relu).then_inc(bank_free[b], 1)
                        act.wait_ge(to_round, 4 * q + rounds.n + jj + 1)
                        round_to(hid_hi[:, bass.ds(4 * q + jj, 1), :],
                                 relu2[jj % 2][:, :].rearrange("p (a s) -> p a s", a=1))
                rounds.n += HALF
                for f in range(2):
                    for g in range(GROUP):
                        n = n0 + HALF + f * GROUP + g
                        if n + AHEAD < BLOCKS:
                            split(n + AHEAD)
                    if half == 1:
                        for t in range(TT):
                            b = FF2_BANKS[half][f][t]
                            act.wait_ge(bank_free[b], ffn_uses[half][f][t] + 1)
                            if 4 * f + t:
                                act.wait_ge(half_sums, 4 * f + t)
                            act.activation(relu[t % 2][:, :], x1[:, t, f * S:(f + 1) * S], ACT.Square,
                                           accum_out=ssq[:, 4 * f + t:4 * f + t + 1]).then_inc(half_sums, 1)

        @block.vector
        def _(dve):
            rounded, steps, freed_by_self = Tally(), Tally(), Tally()

            def link(ins):
                ins.then_inc(vec_step, 1)
                dve.wait_ge(vec_step, steps.next())

            def past(counter, value):
                if value > 0:
                    dve.wait_ge(counter, value)

            def split(n, per=0, i=0):
                s = slots[n]
                dve.wait_ge(hi_split, per * i + n + 1)
                dve.tensor_tensor(w_lo[s][:, :], w_raw[s][:, :], r32(w_hi[s][:, :]), ALU.subtract)\
                    .then_inc(lo_split, 1)

            def rest(dst, src, hi, scale=None):
                dve.wait_ge(hi_written, rounded.next())
                if scale is None:
                    return dve.tensor_tensor(dst, src, r32(hi), ALU.subtract)
                return dve.scalar_tensor_tensor(out=dst, in0=src, scalar=scale, in1=r32(hi),
                                                op0=ALU.mult, op1=ALU.subtract)

            def norm_rows(s, gain):
                dve.wait_ge(squares_summed, s + 1)
                dve.tensor_scalar(msq[:, s:s + 1], ssq[:, s:s + 1], 1.0 / D, EPS, ALU.mult, ALU.add)\
                    .then_inc(msq_set, 1)
                dve.wait_ge(rms_set, s + 1)
                dve.scalar_tensor_tensor(out=stage[s][:, :], in0=stage[s][:, :], scalar=rms[:, s:s + 1],
                                         in1=gain[:, :], op0=ALU.mult, op1=ALU.mult).then_inc(normed, 1)

            def log_sigmoid():
                dve.wait_ge(late_in, LATE)
                link(dve.tensor_scalar(lg_work[:, :], logit[:, :], -1.0, None, ALU.mult))
                dve.tensor_tensor(lg_work[:, :], lg_work[:, :], logit[:, :], ALU.min).then_inc(logit_abs, 1)
                dve.wait_ge(logit_exp, 1)
                link(dve.tensor_scalar(lg_z[:, :], exp_abs[:, :], 2.0, None, ALU.add))
                link(dve.reciprocal(lg_z[:, :], lg_z[:, :]))
                link(dve.tensor_tensor(lg_z[:, :], lg_z[:, :], exp_abs[:, :], ALU.mult))
                link(dve.tensor_tensor(lg_z2[:, :], lg_z[:, :], lg_z[:, :], ALU.mult))
                link(dve.tensor_scalar(log_g[:, :], lg_z2[:, :], 1.0 / 17, None, ALU.mult))
                for odd in range(15, 0, -2):
                    link(dve.scalar_tensor_tensor(out=log_g[:, :], in0=log_g[:, :], scalar=1.0 / odd,
                                                  in1=(lg_z2 if odd > 1 else lg_z)[:, :],
                                                  op0=ALU.add, op1=ALU.mult))
                link(dve.tensor_scalar(lg_work[:, :], logit[:, :], 0.0, None, ALU.min))
                link(dve.scalar_tensor_tensor(out=log_g[:, :], in0=log_g[:, :], scalar=-2.0,
                                              in1=lg_work[:, :], op0=ALU.mult, op1=ALU.add))

            def window_means(i, b):
                dve.wait_ge(pads_set, 1)
                p = padded[0]
                dve.wait_ge(blocks_done, pool_block[i] + 1)
                ins = dve.tensor_copy(p[:, PAD:PAD + S], bank[b][:, :])
                ins.then_inc(bank_free[b], 1)
                dve.wait_ge(bank_free[b], banks_of["pool", i][0][1] + 1)
                src, dst, width = padded[1], padded[2], S + 2 * PAD
                past(mixed, i)
                link(dve.tensor_tensor(src[:, 1:width], p[:, 1:width], p[:, 0:width - 1], ALU.add))
                lo, hi, reach = 1, width, 1
                for _ in range(i):
                    lo, hi = lo + reach, hi - reach
                    link(dve.tensor_tensor(dst[:, lo:hi], src[:, lo + reach:hi + reach],
                                           src[:, lo - reach:hi - reach], ALU.add))
                    src, dst, reach = dst, src, 2 * reach
                link(dve.tensor_tensor(work_a[:, :], src[:, PAD:PAD + S], counts[:, i, :], ALU.mult))
                dve.tensor_tensor(work_a[:, :], work_a[:, :], p[:, PAD:PAD + S], ALU.subtract).then_inc(to_round, 1)
                rest(mix_lo[:, :], work_a[:, :], mix_hi[:, :]).then_inc(mixed, 1)

            dve.wait_ge(early_in, 48)
            norm_rows(0, gain_mem)
            norm_rows(1, gain_mem)
            for kind, i, n, banks in STEPS:
                b = banks[0][0]
                if (kind, i) == ("mem_k", 0):
                    for first in range(AHEAD):
                        split(first)
                if kind in BLOCK_STEPS:
                    for more in range(2 if kind == "v" else 1):
                        split(n + AHEAD + more)
                if kind == "turn":
                    hi, lo = (memT_hi, memT_lo) if i < MT else (h_hi, h_lo)
                    tok = slice(i * P, (i + 1) * P) if i < MT else slice((i - MT) * P, (i - MT + 1) * P)
                    for c, (b, _) in enumerate(banks):
                        rest(lo[:, 4 * c:4 * c + 4, tok], bank[b][:, :].rearrange("p (k n) -> p k n", n=P),
                             hi[:, 4 * c:4 * c + 4, tok]).then_inc(bank_free[b], 1)
                elif kind == "mem_k":
                    rest(memK_lo[:, i, :], bank[b][:, 0:M], memK_hi[:, i, :]).then_inc(bank_free[b], 1)
                    norm_rows(MT + i, gain_x)
                elif kind == "mem_v" and i == 3:
                    for t in range(MT):
                        b = banks[t][0]
                        rest(memV_lo[:, t, :], bank[b][:, :], memV_hi[:, t, :]).then_inc(bank_free[b], 1)
                elif kind == "mem_q":
                    if i == 0:
                        log_sigmoid()
                        dve.wait_ge(grp_rounded, 1)
                        dve.tensor_tensor(grp_lo[:, :, :], grp_raw[:, :, :], r32(grp_hi[:, :, :]), ALU.subtract)\
                            .then_inc(grp_split, 1)
                    rest(mq_lo[:, i, :], bank[b][:, :], mq_hi[:, i, :]).then_inc(bank_free[b], 1)
                elif kind == "pool":
                    window_means(i, b)
                elif kind == "mix":
                    rest(pool_lo[:, i, :], bank[b][:, :], pool_hi[:, i, :], pscale[:, i:i + 1]).then_inc(bank_free[b], 1)
                elif kind == "att_s":
                    dve.wait_ge(scores_done, i + 1)
                    for c, (b, _) in enumerate(banks):
                        link(dve.tensor_reduce(row_max[:, 2 * c:2 * c + 2],
                                               bank[b][:, :].rearrange("p (t m) -> p t m", m=M), AX.X, ALU.max))
                    dve.tensor_scalar(row_max[:, 0:4], row_max[:, 0:4], -QK_SCALE, None, ALU.mult).then_inc(max_set, 1)
                    for b, uses in banks:
                        dve.wait_ge(bank_free[b], uses + 1)
                    link(dve.reciprocal(row_inv[:, 0:4], row_sum[:, 0:4]))
                    for t in range(TT):
                        ins = dve.tensor_scalar(probs[:, t, :], probs[:, t, :], row_inv[:, t:t + 1], None, ALU.mult)
                    ins.then_inc(probs_set, 1)
                elif kind == "att_t":
                    for c, (b, _) in enumerate(banks):
                        rest(probT_lo[:, c, :], bank[b][:, :], probT_hi[:, c, :]).then_inc(bank_free[b], 1)
                elif kind == "att_o":
                    rest(att_lo[:, i, :], bank[b][:, :], att_hi[:, i, :]).then_inc(bank_free[b], 1)
                elif kind in ("q", "k"):
                    turn = 2 * i + (kind == "k")
                    dve.wait_ge(halves_swapped, turn + 1)
                    past(mixed, 4)
                    past(qk_ready, turn)
                    past(s_ready, 4 * i)
                    past(ret_ready, 2 * i if kind == "k" else 2 * i - 2)
                    dve.tensor_tensor(work_a[:, :], bank[b][:, :], cos[:, :], ALU.mult).then_inc(bank_free[b], 1)
                    dve.wait_ge(bank_free[b], banks[0][1] + 1)
                    dve.wait_ge(sin_done, turn + 1)
                    dve.tensor_tensor(work_a[:, :], work_a[:, :], work_b[:, :], ALU.add).then_inc(to_round, 1)
                    c = int(kind == "k")
                    rest(qk_lo[:, c, :], work_a[:, :], qk_hi[:, c, :]).then_inc(qk_ready, 1)
                    if kind == "q":
                        if i:
                            dve.wait_ge(ret_values_done, i)
                        dve.tensor_scalar(decay_a[:, :], dist[:, :], 0.0, log_g[:, i:i + 1], ALU.max, ALU.mult)
                        link(dve.tensor_scalar(decay_b[:, :], dist[:, :], 0.0, log_g[:, 4 + i:5 + i],
                                               ALU.min, ALU.mult))
                        dve.tensor_tensor(decay_a[:, :], decay_a[:, :], decay_b[:, :], ALU.subtract)\
                            .then_inc(log_decay_set, 1)
                elif kind == "v":
                    for c, (b, _) in enumerate(banks):
                        rest(v_lo[:, 2 * c:2 * c + 2, :], bank[b][:, :].rearrange("p (t e) -> p t e", e=VD),
                             v_hi[:, 2 * c:2 * c + 2, :]).then_inc(bank_free[b], 1)
                elif kind == "g":
                    dve.wait_ge(sigmoid_g, i + 1)
                    dve.tensor_tensor(gate_g[:, i % 2, :], sig_g[:, :], bank[b][:, :], ALU.mult)\
                        .then_inc(bank_free[b], 1)
                elif kind == "ret_s":
                    dve.wait_ge(decay_set, i // 2 + 1)
                    for jj, (b, _) in enumerate(banks):
                        j = 2 * (i % 2) + jj
                        dve.wait_ge(ret_scores_done, 2 * i + jj + 1)
                        past(s_ready, 2 * i)
                        past(qk_ready, 2 * (i // 2) + 2)
                        past(ret_ready, 2 * (i // 2))
                        dve.scalar_tensor_tensor(out=(work_a, work_c)[jj][:, :], in0=bank[b][:, :],
                                                 scalar=QK_SCALE, in1=decay[:, REACH - j * P:REACH - j * P + S],
                                                 op0=ALU.mult, op1=ALU.mult).then_inc(bank_free[b], 1)
                    for jj in range(2):
                        j = 2 * (i % 2) + jj
                        rest(s_lo[:, j, :], (work_a, work_c)[jj][:, :], s_hi[:, j, :]).then_inc(s_ready, 1)
                elif kind == "ret_v":
                    dve.wait_ge(ret_values_done, i + 1)
                    for t in range(TT):
                        ins = dve.bn_stats(stats[:, 6 * t:6 * t + 6],
                                           bank[banks[t // 2][0]][:, (t % 2) * VD:(t % 2 + 1) * VD])
                    link(ins)
                    for t in range(TT):
                        ins = dve.bn_aggr(moments[:, 2 * t:2 * t + 2], stats[:, 6 * t:6 * t + 6])
                    link(ins)
                    dve.tensor_scalar(ret_var[:, 0:4], moments[:, 1:8:2], EPS, None, ALU.add).then_inc(var_set, 1)
                    dve.wait_ge(rstd_set, i + 1)
                    for t in range(TT):
                        b = banks[t // 2][0]
                        ins = dve.tensor_scalar(o_nat[:, t, :], bank[b][:, (t % 2) * VD:(t % 2 + 1) * VD],
                                                moments[:, 2 * t:2 * t + 1], ret_rstd[:, t:t + 1],
                                                ALU.subtract, ALU.mult)
                        if t % 2:
                            ins.then_inc(bank_free[b], 1)
                elif kind == "ret_t":
                    b0, uses = banks_of["g", 2 * i + 1][0]
                    dve.wait_ge(bank_free[b0], uses + 1)
                    for c, (b, _) in enumerate(banks):
                        dve.wait_ge(ret_turned, 2 * i + c + 1)
                        past(s_ready, 4 * i + 4)
                        past(qk_ready, min(2 * i + 3, 2 * HEADS))
                        dve.tensor_tensor((work_a, work_c)[c][:, :], bank[b][:, :], gate_g[:, c, :], ALU.mult)\
                            .then_inc(bank_free[b], 1)
                    for c in range(2):
                        rest(ret_lo[:, 2 * i + c, :], (work_a, work_c)[c][:, :], ret_hi[:, 2 * i + c, :])\
                            .then_inc(ret_ready, 1)

            chain0 = steps.n
            dve.sem_inc(merged_ready, 1)
            with dve.Fori(0, KD) as m:
                for g in range(3):
                    split(MERGE0 + AHEAD + g, 5, m)
                split(MERGE0 + AHEAD + 3, 5, m)
                for g in range(N_BRANCHES):
                    if g < 2:
                        dve.wait_ge(blocks_done, 5 * m + MERGE0 + 4 + g)
                    dve.wait_ge(bank_free[g], m + used_merge[g] + 1)
                    dve.tensor_tensor(sig[g][:, :], sig[g][:, :], bank[3 + g][:, :], ALU.mult)\
                        .then_inc(bank_free[3 + g], 1)
                split(MERGE0 + AHEAD + 4, 5, m)
                for g in (0, 1):
                    dve.wait_ge(bank_free[3 + g], m + used_merge[3 + g] + 1)
                dve.tensor_tensor(sig[0][:, :], sig[0][:, :], sig[1][:, :], ALU.add).then_inc(vec_step, 1)
                dve.wait_ge(vec_step, m + chain0 + 1)
                dve.wait_ge(bank_free[5], m + used_merge[5] + 1)
                dve.tensor_tensor(sig[0][:, :], sig[0][:, :], sig[2][:, :], ALU.add).then_inc(to_round, 1)
                dve.wait_ge(hi_written, m + rounded.n + 1)
                dve.tensor_tensor(mrg_lo[:, bass.ds(m, 1), :], sig[0][:, :].rearrange("p (a s) -> p a s", a=1),
                                  r32(mrg_hi[:, bass.ds(m, 1), :]), ALU.subtract).then_inc(merged_ready, 1)
            steps.n += KD
            rounded.n += KD

            for m in range(KD):
                split(OUT0 + m + AHEAD)
                dve.wait_ge(bank_free[6], used_out[6] + m + 1)
                dve.wait_ge(blocks_done, OUT0 + m + 1)
                dve.tensor_tensor(x1T[:, m, :], bank[m % 2][:, :], x1T[:, m, :], ALU.add)\
                    .then_inc(bank_free[m % 2], 1)
                rest(h2_lo[:, m, :], x1T[:, m, :], h2_hi[:, m, :], gain2[:, m:m + 1]).then_inc(h2_ready, 1)

            for half in range(2):
                n0 = FFN0 + half * FFN_HALF_BLOCKS
                pair = FF1_BANKS[half]
                with dve.Fori(0, HALF // 4) as q:
                    for jj in range(4):
                        b = pair[jj % 2]
                        split(n0 + jj + AHEAD, 4, q)
                        dve.wait_ge(bank_free[b], 2 * q + ff1_uses[half][jj % 2] + jj // 2 + 1)
                        dve.tensor_tensor(relu2[jj % 2][:, :], relu[jj % 2][:, :], relu[jj % 2][:, :], ALU.mult)\
                            .then_inc(to_round, 1)
                        dve.wait_ge(hi_written, 4 * q + rounded.n + jj + 1)
                        dve.tensor_tensor(hid_lo[:, bass.ds(4 * q + jj, 1), :],
                                          relu2[jj % 2][:, :].rearrange("p (a s) -> p a s", a=1),
                                          r32(hid_hi[:, bass.ds(4 * q + jj, 1), :]), ALU.subtract)\
                            .then_inc(hid_ready, 1)
                rounded.n += HALF
                if half == 0:
                    dve.wait_ge(ms_done, 1)
                    dve.tensor_scalar(msq[:, 0:4], bank[2][:, 0:4], EPS, None, ALU.add).then_inc(bank_free[2], 1)
                    dve.wait_ge(bank_free[2], used_out[2] + 1)
                    link(dve.reciprocal(inv_ms[:, 0:4], msq[:, 0:4]))
                    dve.wait_ge(bank_free[7], used_out[7] + KD)
                for f in range(2):
                    four, uses = FF2_BANKS[half][f], ffn_uses[half][f]
                    for g in range(GROUP):
                        n = n0 + HALF + f * GROUP + g
                        if n + AHEAD < BLOCKS:
                            split(n + AHEAD)
                    dve.wait_ge(blocks_done, n0 + HALF + (f + 1) * GROUP)
                    for t in range(TT):
                        if half:
                            dve.wait_ge(bank_free[FF2_BANKS[0][f][t]], ffn_uses[0][f][t] + 1)
                        part = x1[:, t, f * S:(f + 1) * S]
                        dve.scalar_tensor_tensor(out=part, in0=bank[four[t]][:, :], scalar=inv_ms[:, t:t + 1],
                                                 in1=part, op0=ALU.mult, op1=ALU.add).then_inc(bank_free[four[t]], 1)

            dve.wait_ge(gain_in, 16)
            for t in range(TT):
                dve.wait_ge(half_sums, TT + t + 1)
                link(dve.tensor_tensor(msq[:, t:t + 1], ssq[:, t:t + 1], ssq[:, 4 + t:5 + t], ALU.add))
                dve.tensor_scalar(msq[:, t:t + 1], msq[:, t:t + 1], 1.0 / D, EPS, ALU.mult, ALU.add)\
                    .then_inc(msq_set, 1)
            for t in range(TT):
                dve.wait_ge(rms_set, MT + TT + t + 1)
                dve.scalar_tensor_tensor(out=y[t][:, :], in0=x1[:, t, :], scalar=rms[:, t:t + 1],
                                         in1=gain_f[:, :], op0=ALU.mult, op1=ALU.mult).then_inc(y_ready, 1)

        @block.gpsimd
        def _(pool):
            pool.memset(minus_half[:, :], -0.5).then_inc(consts_set, 1)
            pool.memset(mean_col[:, :], 1.0 / D).then_inc(consts_set, 1)
            pool.wait_ge(consts_set, 2)

            def inv_sqrt(dst, src, width):
                return pool.tensor_tensor(dst, src, minus_half[:, 0:width], ALU.pow)

            for s in range(MT + TT):
                pool.wait_ge(msq_set, s + 1)
                inv_sqrt(rms[:, s:s + 1], msq[:, s:s + 1], 1).then_inc(rms_set, 1)
            for b, uses in banks_of["turn", MT + 2] + banks_of["turn", MT + 3]:
                pool.wait_ge(bank_free[b], uses + 1)
            pool.memset(padded[0][:, :], 0.0).then_inc(pads_set, 1)

            for kind, i, n, banks in STEPS:
                if kind in ("q", "k"):
                    turn = 2 * i + (kind == "k")
                    pool.wait_ge(halves_swapped, turn + 1)
                    if turn:
                        pool.wait_ge(qk_ready, turn)
                    pool.tensor_tensor(work_b[:, :], swapped[:, :], sin[:, :], ALU.mult).then_inc(sin_done, 1)
                elif kind == "ret_v":
                    pool.wait_ge(var_set, i + 1)
                    inv_sqrt(ret_rstd[:, 0:4], ret_var[:, 0:4], 4).then_inc(rstd_set, 1)

            for m in range(1, KD):
                pool.wait_ge(square_set, m + 1)
                if m > 1:
                    pool.wait_ge(sumsq_set, m - 1)
                pool.tensor_tensor(sumsq[:, :], sumsq[:, :], square[m % 2][:, :], ALU.add).then_inc(sumsq_set, 1)

            for t in range(TT):
                pool.wait_ge(msq_set, MT + TT + t + 1)
                inv_sqrt(rms[:, t:t + 1], msq[:, t:t + 1], 1).then_inc(rms_set, 1)


_INS = ["x", "mem", "w_in", "ret_decay_logit", "w_ret_o", "w_pool_grp", "pool_scale", "w_pool_o",
        "w_mem_kv", "w_mem_o", "w_out", "w_ff1", "w_ff2", "norm1_g", "norm2_g", "mem_norm_g",
        "final_norm_g"]


def shape_tables():
    f32 = np.float32
    inv = (f32(10000.0) ** (-np.arange(0, P, 2, dtype=f32) / f32(P))).astype(f32)
    angle = (np.arange(S, dtype=f32)[None, :] * inv[:, None]).astype(f32)
    cos, sin = np.cos(angle).astype(f32), np.sin(angle).astype(f32)
    distance = np.arange(SPAN)[None, :] - np.arange(P)[:, None] - REACH
    n = np.arange(S)
    counts = [1.0 / (np.clip(n + w // 2, 0, S) - np.clip(n - w // 2, 0, S)) for w in POOL_WINDOWS]
    return {
        "identity": np.eye(P, dtype=f32),
        "cos_table": np.concatenate([cos, cos]),
        "sin_table": np.concatenate([-sin, sin]),
        "distance": distance.astype(f32),
        "inv_count": np.concatenate(counts)[None, :].astype(f32),
    }


def kernel(**inputs):
    import concourse.bacc as bacc
    from concourse.bass_utils import run_bass_kernel_spmd

    nc = bacc.Bacc("TRN2", target_bir_lowering=False, num_devices=1)
    arrays, args = {}, []
    given = {name: np.ascontiguousarray(inputs[name]) for name in _INS}
    for name, a in {**given, **shape_tables()}.items():
        arrays[f"in_{name}"] = a
        args.append(nc.dram_tensor(f"in_{name}", a.shape, mybir.dt.from_np(a.dtype), kind="ExternalInput").ap())
    out = nc.dram_tensor("out", (1, S, D), FP32, kind="ExternalOutput").ap()
    encoder_kernel(nc, *args, out)
    result = run_bass_kernel_spmd(nc, [arrays], core_ids=[0])
    return result.results[0]["out"]
```

```python
from contextlib import ExitStack

import numpy as np
import concourse.bass as bass
from concourse import mybir

FP32 = mybir.dt.float32
FP32R = mybir.dt.float32r
ALU = mybir.AluOpType
ACT = mybir.ActivationFunctionType
AX = mybir.AxisListType

P = 128
D = 1024
S = 512
KD = D // P
TT = S // P
M = 256
MT = M // P
HEADS = 4
VD = 256
POOL_WINDOWS = (2, 4, 8, 16)
PAD = max(POOL_WINDOWS) // 2
HIDDEN = 4 * D
N_BRANCHES = 3
EPS = 1e-6
QK_SCALE = float(P) ** -0.5
BLOCK = 1024
RING = 5
DEPTH = 4
AHEAD = 2
KB = 1024

COL_Q, COL_K, COL_V, COL_G = 0, 512, 1024, 2048
COL_POOL, COL_MQ, COL_GATES = 3072, 3584, 4096

REACH = S - P
SPAN = REACH + S


def projection_steps():
    order = [("turn", 0), ("turn", 1)]
    order += [("mem_k", h) for h in range(HEADS)]
    for b in range(4):
        order += [("turn", MT + b), ("mem_v", b)]
    order += [("mem_q", 0), ("mem_q", 1), ("att_s", 0), ("mem_q", 2), ("att_t", 0),
              ("mem_q", 3), ("att_o", 0),
              ("pool", 0), ("att_s", 1), ("pool", 1), ("mean", 0), ("att_t", 1),
              ("pool", 2), ("mean", 1), ("mix", 0), ("att_o", 1),
              ("pool", 3), ("mean", 2), ("mix", 1), ("att_s", 2), ("mean", 3)]
    more = {("q", 0): [("mix", 2), ("att_t", 2)], ("k", 0): [("mix", 3), ("att_o", 2)],
            ("v", 0): [("att_s", 3)], ("g", 0): [("att_t", 3)], ("g", 1): [("att_o", 3)]}
    for h in range(HEADS):
        for step in (("q", h), ("k", h), ("v", h), ("g", 2 * h), ("g", 2 * h + 1)):
            order += [step] + more.get(step, [])
            if step[0] == "k" and h > 0:
                order.append(("ret_t", h - 1))
            if step[0] == "v":
                order.append(("ret_s", 2 * h))
            if step == ("g", 2 * h):
                order.append(("ret_s", 2 * h + 1))
            if step == ("g", 2 * h + 1):
                order.append(("ret_v", h))
    order.append(LAST_TURN)

    fixed = {"mem_v": (4, 5), "v": (4, 5), "att_s": (6, 7), "att_t": (6, 7), "att_o": (2,),
             "ret_s": (2, 3), "ret_v": (6, 7), "ret_t": (6, 7), "mean": (), "mix": (3,)}
    blocks_of = {"turn": 0, "att_s": 0, "att_t": 0, "att_o": 0, "mean": 0, "mix": 0, "ret_s": 0,
                 "ret_v": 0, "ret_t": 0, "v": 2}
    used = [0] * 8
    block, projected, steps = 0, 0, []
    for kind, i in order:
        if kind == "turn":
            banks = (6, 7) if i % 2 == 0 else (2, 3)
        elif kind in fixed:
            banks = fixed[kind]
        else:
            banks = (projected % 2,)
            projected += 1
        first = kind != "mem_v" or i == 0
        steps.append((kind, i, block, tuple((b, used[b] - (0 if first else 1)) for b in banks)))
        if first:
            for b in banks:
                used[b] += 1
        block += blocks_of.get(kind, 1)
    return steps, block, used


LAST_TURN = ("ret_t", HEADS - 1)
BLOCK_STEPS = ("mem_k", "mem_v", "mem_q", "pool", "q", "k", "v", "g")
LATE = 16 * 8


class Tally:

    def __init__(self):
        self.n = 0

    def next(self):
        self.n += 1
        return self.n


def slot_of(n, merge_first, merge_blocks):
    if merge_first <= n < merge_first + merge_blocks:
        return (n - merge_first) % 5
    return n % 4


def encoder_kernel(nc, x, mem, w_in, ret_decay_logit, w_ret_o, w_pool_grp, pool_scale, w_pool_o,
                   w_mem_kv, w_mem_o, w_out, w_ff1, w_ff2, norm1_g, norm2_g, mem_norm_g,
                   final_norm_g, identity, cos_table, sin_table, distance, inv_count, out):
    STEPS, MERGE0, USED_A = projection_steps()
    MERGE_BLOCKS = 5 * KD
    OUT0 = MERGE0 + MERGE_BLOCKS
    FFN0 = OUT0 + KD
    HALF = HIDDEN // P // 2
    GROUP = HALF // 2
    FFN_HALF_BLOCKS = HALF + 2 * GROUP
    BLOCKS = FFN0 + 2 * FFN_HALF_BLOCKS
    slots = [slot_of(n, MERGE0, MERGE_BLOCKS) for n in range(BLOCKS)]
    loads = [slots[:n + 1].count(slots[n]) for n in range(BLOCKS)]
    FF1_BANKS = ((0, 1), (2, 3))
    FF2_BANKS = (((2, 3, 4, 5), (6, 7, 0, 1)), ((4, 5, 6, 7), (0, 1, 2, 3)))

    used_merge = list(USED_A)
    used_out = [u + (KD if b < 6 else 0) for b, u in enumerate(used_merge)]
    used_ffn = list(used_out)
    for b, n in ((0, KD // 2), (1, KD // 2), (6, KD + 1), (7, KD)):
        used_ffn[b] += n

    ff1_uses, ffn_uses, at_now = [], [], list(used_ffn)
    for half in range(2):
        ff1_uses.append([at_now[b] for b in FF1_BANKS[half]])
        for b in FF1_BANKS[half]:
            at_now[b] += HALF // 2
        ffn_uses.append([])
        for f in range(2):
            ffn_uses[half].append([at_now[b] for b in FF2_BANKS[half][f]])
            for b in FF2_BANKS[half][f]:
                at_now[b] += 1
    ctx = ExitStack()
    with ctx:
        BASE = 16512

        def at(name, kb, shape, dtype=FP32):
            size = int(np.prod(shape[1:])) * 4
            assert BASE + kb * KB + size <= 229344, name
            return nc.alloc_sbuf_tensor_at(name, shape, dtype, offset=int(BASE + kb * KB))

        def sem(name):
            return ctx.enter_context(nc.semaphore(name))

        h_hi, h_lo = at("h_hi", 0, [P, KD, S], FP32R), at("h_lo", 16, [P, KD, S], FP32R)
        w_hi = [at(f"w_hi{s}", 32 + 4 * s, [P, BLOCK], FP32R) for s in range(RING)]
        w_lo = [at(f"w_lo{s}", 52 + 4 * s, [P, BLOCK], FP32R) for s in range(RING)]
        w_raw = [at(f"w_raw{s}", 72 + 4 * s, [P, BLOCK]) for s in range(RING)]
        swapped, work_a = at("swapped", 48, [P, S]), at("work_a", 50, [P, S])
        work_b, sig_g = at("work_b", 68, [P, S]), at("sig_g", 70, [P, S])
        square_junk, o_nat = at("square_junk", 88, [P, D]), at("o_nat", 88, [P, TT, VD])
        memT_hi, memT_lo = at("memT_hi", 92, [P, KD, M], FP32R), at("memT_lo", 108, [P, KD, M], FP32R)
        memK_hi, memK_lo = at("memK_hi", 100, [P, HEADS, M], FP32R), at("memK_lo", 116, [P, HEADS, M], FP32R)
        memV_hi, memV_lo = at("memV_hi", 104, [P, MT, S], FP32R), at("memV_lo", 120, [P, MT, S], FP32R)
        probT_hi, probT_lo = at("probT_hi", 92, [P, MT, S], FP32R), at("probT_lo", 108, [P, MT, S], FP32R)
        probs = at("probs", 96, [P, TT, M])
        ret_hi, ret_lo = at("ret_hi", 92, [P, KD, S], FP32R), at("ret_lo", 108, [P, KD, S], FP32R)
        mq_hi, mq_lo = at("mq_hi", 124, [P, HEADS, S], FP32R), at("mq_lo", 132, [P, HEADS, S], FP32R)
        att_hi, att_lo = at("att_hi", 124, [P, HEADS, S], FP32R), at("att_lo", 132, [P, HEADS, S], FP32R)
        pool_hi, pool_lo = at("pool_hi", 140, [P, 4, S], FP32R), at("pool_lo", 148, [P, 4, S], FP32R)
        stage = [at(f"stage{s}", 156 + 4 * s, [P, D]) for s in range(MT + TT)]
        grp_raw = at("grp_raw", 68, [P, 4, P])
        grp_hi, grp_lo = at("grp_hi", 70, [P, 4, P], FP32R), at("grp_lo", 205, [P, 4, P], FP32R)
        mix_hi = [at(f"mix_hi{s}", 164 + 2 * s, [P, S], FP32R) for s in range(2)]
        mix_lo = [at(f"mix_lo{s}", 168 + 2 * s, [P, S], FP32R) for s in range(2)]
        padded = [at("padded_even", 156, [P, S + 2 * PAD]), at("padded_odd", 172, [P, S + 2 * PAD])]
        sums = [at(f"sums{s}", 174.125 + 2.125 * s, [P, S + 2 * PAD]) for s in range(2)]
        counts = at("counts", 180, [P, 4, S])
        qk_hi, qk_lo = at("qk_hi", 156, [P, 2, S], FP32R), at("qk_lo", 160, [P, 2, S], FP32R)
        v_hi, v_lo = at("v_hi", 164, [P, TT, VD], FP32R), at("v_lo", 168, [P, TT, VD], FP32R)
        s_hi, s_lo = at("s_hi", 172, [P, TT, S], FP32R), at("s_lo", 180, [P, TT, S], FP32R)
        decay_a, decay_b = at("decay_a", 172, [P, SPAN]), at("decay_b", 176, [P, SPAN])
        mrg_hi, mrg_lo = at("mrg_hi", 156, [P, KD, S], FP32R), at("mrg_lo", 172, [P, KD, S], FP32R)
        ident = at("ident", 188, [P, P])
        cos, sin = at("cos", 189, [P, S]), at("sin", 191, [P, S])
        dist, decay = at("dist", 193, [P, SPAN]), at("decay", 197, [P, SPAN])
        gate_g, work_c = at("gate_g", 201, [P, 2, S]), at("work_c", 205, [P, S])
        gain_x, gain_mem = at("gain_x", 197, [P, D]), at("gain_mem", 201, [P, D])
        gain_rows, ones_row = at("gain_rows", 16, [1, 2, D]), at("ones_row", 24, [1, P])
        sig = [at("sig_ret", 189, [P, S]), at("sig_pool", 191, [P, S]), at("sig_mem", 193, [P, S])]
        x_cols = [at(f"x_cols{s}", 197 + 2 * s, [P, TT, P]) for s in range(4)]
        sumsq, square = at("sumsq", 205, [P, S]), [at("square0", 2, [P, S]), at("square1", 4, [P, S])]
        h2_hi, h2_lo = at("h2_hi", 92, [P, KD, S], FP32R), at("h2_lo", 108, [P, KD, S], FP32R)
        x1T, x1 = at("x1T", 124, [P, KD, S]), at("x1", 140, [P, TT, D])
        hid_hi, hid_lo = at("hid_hi", 0, [P, HALF, S], FP32R), at("hid_lo", 156, [P, HALF, S], FP32R)
        relu = [at("relu0", 189, [P, S]), at("relu1", 191, [P, S])]
        relu2 = [at("relu2_0", 193, [P, S]), at("relu2_1", 195, [P, S])]
        gain_f = at("gain_f", 197, [P, D])
        y = [at(f"y{t}", 92 + 4 * t, [P, D]) for t in range(TT)]
        x2g = at("x2g", 108, [P, TT, S])

        taken = [0]

        def tiny(name, n):
            taken[0] += n
            assert taken[0] <= 192
            return at(name, 207 + (taken[0] - n) * 4 / KB, [P, n])

        ssq, msq, rms = tiny("ssq", 8), tiny("msq", 8), tiny("rms", 8)
        minus_half, mean_col = tiny("minus_half", 8), tiny("mean_col", 8)
        logit, lg_work, exp_abs = tiny("logit", 8), tiny("lg_work", 8), tiny("exp_abs", 8)
        lg_z, lg_z2, log_g = tiny("lg_z", 8), tiny("lg_z2", 8), tiny("log_g", 8)
        pscale, gain2 = tiny("pscale", 8), tiny("gain2", 8)
        row_max, row_sum, row_inv = tiny("row_max", 8), tiny("row_sum", 8), tiny("row_inv", 8)
        ret_var, ret_rstd = tiny("ret_var", 8), tiny("ret_rstd", 8)
        stats, moments = tiny("stats", 24), tiny("moments", 8)
        inv_ms, half_mean = tiny("inv_ms", 8), tiny("half_mean", 8)

        bank = [ctx.enter_context(nc.psum_tensor(f"bank{b}", [P, S], FP32)) for b in range(8)]

        stage_in = [sem(f"stage_in{s}") for s in range(MT + TT)]
        ident_in, late_in, gain_in = sem("ident_in"), sem("late_in"), sem("gain_in")
        gain_row_in = [sem("gain_row_in_mem"), sem("gain_row_in_x")]
        gains_spread, gains_copied = sem("gains_spread"), sem("gains_copied")
        grp_rounded, grp_split, mix_done = sem("grp_rounded"), sem("grp_split"), sem("mix_done")
        raw_in = [sem(f"raw_in{s}") for s in range(RING)]
        x_cols_in = [sem(f"x_cols_in{s}") for s in range(4)]
        stored, slots_cleared = sem("stored"), sem("slots_cleared")
        hi_split, lo_split = sem("hi_split"), sem("lo_split")
        blocks_done = sem("blocks_done")
        bank_free = [sem(f"bank_free{b}") for b in range(8)]
        hi_written = sem("hi_written")
        to_round = sem("to_round")
        consts_set = sem("consts_set")
        squares_summed, msq_set, rms_set = sem("squares_summed"), sem("msq_set"), sem("rms_set")
        normed = sem("normed")
        turned = sem("turned")
        scores_done, probs_turned, att_done = sem("scores_done"), sem("probs_turned"), sem("att_done")
        max_set, probs_set = sem("max_set"), sem("probs_set")
        logit_abs, logit_exp = sem("logit_abs"), sem("logit_exp")
        mixed, pads_set = sem("mixed"), sem("pads_set")
        sums_done = sem("sums_done")
        halves_swapped, sin_done = sem("halves_swapped"), sem("sin_done")
        qk_ready = sem("qk_ready")
        log_decay_set, decay_set = sem("log_decay_set"), sem("decay_set")
        ret_scores_done, s_ready, ret_values_done = sem("ret_scores_done"), sem("s_ready"), sem("ret_values_done")
        var_set, rstd_set = sem("var_set"), sem("rstd_set")
        ret_turned, ret_ready = sem("ret_turned"), sem("ret_ready")
        sigmoid_g = sem("sigmoid_g")
        merged_ready = sem("merged_ready")
        x_turned, x1_turned, square_set, sumsq_set = sem("x_turned"), sem("x1_turned"), sem("square_set"), sem("sumsq_set")
        h2_ready, hid_ready = sem("h2_ready"), sem("hid_ready")
        ms_done = sem("ms_done")
        half_sums, tokens_done = sem("half_sums"), sem("tokens_done")
        y_ready = [sem("y_ready0"), sem("y_ready1")]
        vec_step, pool_step = sem("vec_step"), sem("pool_step")

        banks_of = {(kind, i): banks for kind, i, _, banks in STEPS}

        w_in_v = w_in.rearrange("l (k p) n -> (l p) k n", p=P)
        kv_v = w_mem_kv.rearrange("l (k p) n -> (l p) k n", p=P)
        ret_o_v = w_ret_o.rearrange("l (k p) n -> (l p) k n", p=P)
        pool_o_v = w_pool_o.rearrange("l (k p) n -> (l p) k n", p=P)
        mem_o_v = w_mem_o.rearrange("l (k p) n -> (l p) k n", p=P)
        out_v = w_out.rearrange("l (k p) n -> (l p) k n", p=P)
        ff1_v = w_ff1.rearrange("l (k p) n -> (l p) k n", p=P)
        ff2_v = w_ff2.rearrange("l (k p) n -> (l p) k n", p=P)
        x_v = x.rearrange("b (t p) d -> (b p) t d", p=P)
        mem_v = mem.rearrange("b (t p) d -> (b p) t d", p=P)
        y_v = out.rearrange("b (t p) d -> (b p) t d", p=P)

        def r32(ap):
            return ap.bitcast(FP32)

        block = ctx.enter_context(nc.Block())

        @block.sync
        def _(sp):
            def load(n, view, k0, k1, col, width, turn=0):
                if n >= DEPTH:
                    sp.wait_ge(lo_split, turn + n - DEPTH + 1)
                    if not isinstance(turn, int):
                        sp.sem_inc(slots_cleared, 1)
                sp.dma_start(w_raw[slots[n]][:, :].rearrange("p (k n) -> p k n", n=width),
                             view[:, k0:k1, bass.ds(col, width)]).then_inc(raw_in[slots[n]], 16)

            def load_constants():
                for dst, src in (
                    (pscale[:, 0:4], pool_scale.rearrange("l (g c) -> c (l g)", c=P)),
                    (gain2[:, :], norm2_g.rearrange("l (k c) -> c (l k)", c=P)),
                    (logit[:, :], ret_decay_logit.rearrange("l a h -> l (a h)").broadcast_to([P, 8])),
                    (grp_raw[:, :, :], w_pool_grp.rearrange("l g c d -> (l c) g d")),
                    (cos[:, :], cos_table), (sin[:, :], sin_table), (dist[:, :], distance),
                    (counts[:, :, :].rearrange("p g s -> p (g s)"), inv_count.broadcast_to([P, 4 * S])),
                ):
                    sp.dma_start(dst, src, allow_slow_non_contiguous=True).then_inc(late_in, 16)

            sp.dma_start(gain_rows[:, 0, :], mem_norm_g.rearrange("(a n) -> a n", a=1)).then_inc(gain_row_in[0], 16)
            sp.dma_start(stage[0][:, :], mem_v[:, 0, :]).then_inc(stage_in[0], 16)
            sp.dma_start(ident[:, :], identity).then_inc(ident_in, 16)
            sp.dma_start(gain_rows[:, 1, :], norm1_g).then_inc(gain_row_in[1], 16)
            sp.dma_start(stage[1][:, :], mem_v[:, 1, :]).then_inc(stage_in[1], 16)

            for kind, i, n, _ in STEPS:
                if kind == "mem_k":
                    load(n, kv_v, 0, KD, i * P, P)
                    if i in (1, 3):
                        for t in (i - 1, i):
                            sp.dma_start(stage[MT + t][:, :], x_v[:, t, :]).then_inc(stage_in[MT + t], 16)
                    if i == 3:
                        load_constants()
                elif kind == "mem_v":
                    load(n, kv_v, 2 * i, 2 * i + 2, HEADS * P, S)
                elif kind == "v":
                    load(n, w_in_v, 0, 4, COL_V + i * VD, VD)
                    load(n + 1, w_in_v, 4, KD, COL_V + i * VD, VD)
                elif kind in ("mem_q", "pool", "q", "k", "g"):
                    col = {"mem_q": COL_MQ, "pool": COL_POOL, "q": COL_Q, "k": COL_K, "g": COL_G}[kind]
                    load(n, w_in_v, 0, KD, col + i * P, P)

            def load_gates(m, shift, turn):
                for b in range(N_BRANCHES):
                    load(MERGE0 + 5 * shift + b, w_in_v, 0, KD, COL_GATES + b * D + m * P, P, turn)
                load(MERGE0 + 5 * shift + 3, ret_o_v, 0, KD, m * P, P, turn)

            def load_pool_mem(m, turn):
                n = MERGE0 + 4
                sp.wait_ge(lo_split, turn + n - DEPTH + 1)
                if not isinstance(turn, int):
                    sp.sem_inc(slots_cleared, 1)
                raw = w_raw[slots[n]]
                sp.dma_start(raw[:, 0:S].rearrange("p (k n) -> p k n", n=P),
                             pool_o_v[:, :, bass.ds(m * P, P)]).then_inc(raw_in[slots[n]], 16)
                sp.dma_start(raw[:, S:BLOCK].rearrange("p (k n) -> p k n", n=P),
                             mem_o_v[:, :, bass.ds(m * P, P)]).then_inc(raw_in[slots[n]], 16)

            load_gates(0, 0, 0)
            sp.wait_ge(ret_ready, KD)
            with sp.Fori(0, KD - 1) as m:
                load_pool_mem(m, 5 * m)
                load_gates(m + 1, 1, 5 * m)
            load_pool_mem(KD - 1, 5 * (KD - 1))

            for s in range(4):
                sp.dma_start(x_cols[s][:, :, :], x_v[:, :, s * P:(s + 1) * P]).then_inc(x_cols_in[s], 16)
            for m in range(KD):
                load(OUT0 + m, out_v, 0, KD, m * P, P)
                if m >= 4:
                    sp.wait_ge(x_turned, m - 3)
                    sp.dma_start(x_cols[m - 4][:, :, :], x_v[:, :, m * P:(m + 1) * P]).then_inc(x_cols_in[m - 4], 16)

            for half in range(2):
                n0 = FFN0 + half * FFN_HALF_BLOCKS
                with sp.Fori(0, HALF // 4) as q:
                    for jj in range(4):
                        load(n0 + jj, ff1_v, 0, KD, q * (4 * P) + (half * HALF + jj) * P, P, 4 * q)
                if half == 0:
                    sp.wait_ge(x_turned, KD)
                    sp.dma_start(gain_f[:, :], final_norm_g.rearrange("(a n) -> a n", a=1).broadcast_to([P, D]))\
                        .then_inc(gain_in, 16)
                for f in range(2):
                    for b in range(GROUP):
                        k = half * HALF + 2 * b
                        load(n0 + HALF + f * GROUP + b, ff2_v, k, k + 2, f * S, S)

            for t in range(TT):
                sp.wait_ge(y_ready[0], t + 1)
                sp.wait_ge(y_ready[1], t + 1)
                sp.dma_start(y_v[:, t, :], y[t][:, :]).then_inc(stored, 16)
            sp.wait_ge(stored, 16 * TT)

        @block.tensor
        def _(pe):
            def three(out_ap, wh, wl, xh, xl, first, last):
                pe.matmul(out_ap, wh, xh, start=first, stop=False)
                pe.matmul(out_ap, wh, xl, start=False, stop=False)
                return pe.matmul(out_ap, wl, xh, start=False, stop=last)

            def project(s, out_ap, x_hi, x_lo, tiles, w0=0, tiles_ready=None, before=0):
                for k in range(tiles):
                    if tiles_ready is not None:
                        pe.wait_ge(tiles_ready, before + k + 1)
                    c = slice((w0 + k) * P, (w0 + k + 1) * P)
                    last = three(out_ap, w_hi[s][:, c], w_lo[s][:, c], x_hi[:, k, :], x_lo[:, k, :],
                                 k == 0, k == tiles - 1)
                return last

            def free(b, uses):
                if uses:
                    pe.wait_ge(bank_free[b], uses)

            def read_out(kind, i):
                for b, uses in banks_of[kind, i]:
                    pe.wait_ge(bank_free[b], uses + 1)

            def turn_back_head(i, banks):
                read_out("ret_v", i)
                for c in range(2):
                    for t in range(TT):
                        last = pe.transpose(bank[banks[c][0]][:, t * P:(t + 1) * P],
                                            o_nat[:, t, c * P:(c + 1) * P], ident[:, :])
                    last.then_inc(ret_turned, 1)

            def spread_gain(g, c):
                pe.wait_ge(gain_row_in[g], 16)
                pe.matmul(bank[4 * g + c][:, :], ones_row[:, :], gain_rows[:, g, c * S:(c + 1) * S],
                          start=True, stop=True).then_inc(gains_spread, 1)

            pe.wait_ge(consts_set, 3)
            spread_gain(0, 0)
            spread_gain(0, 1)
            spread_gain(1, 0)
            pe.wait_ge(ident_in, 16)
            for kind, i, n, banks in STEPS:
                if (kind, i) == LAST_TURN:
                    continue
                for b, uses in banks:
                    if kind != "mem_v" or i == 0:
                        free(b, uses)
                if kind == "turn":
                    pe.wait_ge(normed, i + 1)
                    for c, (b, _) in enumerate(banks):
                        for k in range(4):
                            f = (4 * c + k) * P
                            last = pe.transpose(bank[b][:, k * P:(k + 1) * P], stage[i][:, f:f + P], ident[:, :])
                        last.then_inc(turned, 1)
                    if i == 0:
                        spread_gain(1, 1)
                elif kind == "mem_k":
                    pe.wait_ge(lo_split, n + 1)
                    if i == 0:
                        pe.wait_ge(gains_copied, 2)
                        for t in range(MT):
                            read_out("turn", t)
                    project(slots[n], bank[banks[0][0]][:, 0:M], memT_hi, memT_lo, KD).then_inc(blocks_done, 1)
                elif kind == "mem_v":
                    pe.wait_ge(lo_split, n + 1)
                    if i == 0:
                        pe.wait_ge(gains_copied, 4)
                    for t in range(MT):
                        for kk in range(2):
                            k = 2 * i + kk
                            c = slice(kk * S, (kk + 1) * S)
                            tok = slice(t * P, (t + 1) * P)
                            last = three(bank[banks[t][0]][:, :], memT_hi[:, k, tok], memT_lo[:, k, tok],
                                         w_hi[slots[n]][:, c], w_lo[slots[n]][:, c], k == 0, k == KD - 1)
                    last.then_inc(blocks_done, 1)
                elif kind in ("mem_q", "pool", "q", "k", "g"):
                    pe.wait_ge(lo_split, n + 1)
                    if kind == "mem_q" and i == 0:
                        for t in range(MT, MT + TT):
                            read_out("turn", t)
                    project(slots[n], bank[banks[0][0]][:, :], h_hi, h_lo, KD).then_inc(blocks_done, 1)
                elif kind == "v":
                    pe.wait_ge(lo_split, n + 2)
                    for t in range(TT):
                        tok = slice(t * P, (t + 1) * P)
                        dst = bank[banks[t // 2][0]][:, (t % 2) * VD:(t % 2 + 1) * VD]
                        for k in range(KD):
                            s, c = slots[n + k // 4], slice((k % 4) * VD, (k % 4 + 1) * VD)
                            last = three(dst, h_hi[:, k, tok], h_lo[:, k, tok], w_hi[s][:, c], w_lo[s][:, c],
                                         k == 0, k == KD - 1)
                            if t == TT - 1 and k == KD - 2:
                                last.then_inc(blocks_done, 1)
                    last.then_inc(blocks_done, 1)
                elif kind == "mix":
                    pe.wait_ge(mixed, i + 1)
                    pe.wait_ge(grp_split, 1)
                    b = banks[0][0]
                    three(bank[b][:, :], grp_hi[:, i, :], grp_lo[:, i, :], mix_hi[i % 2][:, :],
                          mix_lo[i % 2][:, :], True, True).then_inc(mix_done, 1)
                elif kind == "att_s":
                    read_out("mem_q", i)
                    for t in range(TT):
                        tok = slice(t * P, (t + 1) * P)
                        last = three(bank[banks[t // 2][0]][:, (t % 2) * M:(t % 2 + 1) * M],
                                     mq_hi[:, i, tok], mq_lo[:, i, tok], memK_hi[:, i, :], memK_lo[:, i, :],
                                     True, True)
                    last.then_inc(scores_done, 1)
                elif kind == "att_t":
                    pe.wait_ge(probs_set, i + 1)
                    for c in range(MT):
                        for t in range(TT):
                            last = pe.transpose(bank[banks[c][0]][:, t * P:(t + 1) * P],
                                                probs[:, t, c * P:(c + 1) * P], ident[:, :])
                    last.then_inc(probs_turned, 1)
                elif kind == "att_o":
                    if i == 0:
                        read_out("mem_v", 0)
                    read_out("att_t", i)
                    for c in range(MT):
                        d = slice(i * P, (i + 1) * P)
                        last = three(bank[banks[0][0]][:, :], memV_hi[:, c, d], memV_lo[:, c, d],
                                     probT_hi[:, c, :], probT_lo[:, c, :], c == 0, c == MT - 1)
                    last.then_inc(att_done, 1)
                elif kind == "ret_s":
                    hd, p = i // 2, i % 2
                    pe.wait_ge(qk_ready, 2 * hd + 2)
                    for jj in range(2):
                        j = 2 * p + jj
                        last = three(bank[banks[jj][0]][:, :], qk_hi[:, 1, j * P:(j + 1) * P],
                                     qk_lo[:, 1, j * P:(j + 1) * P], qk_hi[:, 0, :], qk_lo[:, 0, :], True, True)
                        last.then_inc(ret_scores_done, 1)
                elif kind == "ret_v":
                    pe.wait_ge(s_ready, 4 * i + 4)
                    read_out("v", i)
                    for t in range(TT):
                        tok = slice(t * P, (t + 1) * P)
                        for j in range(TT):
                            last = three(bank[banks[t // 2][0]][:, (t % 2) * VD:(t % 2 + 1) * VD],
                                         s_hi[:, j, tok], s_lo[:, j, tok], v_hi[:, j, :], v_lo[:, j, :],
                                         j == 0, j == TT - 1)
                    last.then_inc(ret_values_done, 1)
                elif kind == "ret_t":
                    turn_back_head(i, banks)

            for i in range(4):
                read_out("mix", i)
                read_out("att_o", i)
            def merge_tile(m, first=False):
                for g in range(N_BRANCHES):
                    pe.wait_ge(lo_split, 5 * m + MERGE0 + g + 1)
                    pe.wait_ge(bank_free[g], m + used_merge[g])
                    project(g, bank[g][:, :], h_hi, h_lo, KD).then_inc(blocks_done, 1)
                    if first and g == 0:
                        for b, uses in banks_of[LAST_TURN]:
                            free(b, uses)
                        turn_back_head(HEADS - 1, banks_of[LAST_TURN])
                pe.wait_ge(lo_split, 5 * m + MERGE0 + 4)
                pe.wait_ge(bank_free[3], m + used_merge[3])
                pe.wait_ge(ret_ready, KD)
                project(3, bank[3][:, :], ret_hi, ret_lo, KD).then_inc(blocks_done, 1)
                pe.wait_ge(lo_split, 5 * m + MERGE0 + 5)
                pe.wait_ge(bank_free[4], m + used_merge[4])
                project(4, bank[4][:, :], pool_hi, pool_lo, 4)
                pe.wait_ge(bank_free[5], m + used_merge[5])
                project(4, bank[5][:, :], att_hi, att_lo, 4, 4).then_inc(blocks_done, 1)

            merge_tile(0, first=True)
            with pe.Fori(1, KD) as m:
                merge_tile(m)

            def turn_back(m):
                pe.wait_ge(bank_free[m % 2], used_out[m % 2] + m // 2 + 1)
                free(7, used_out[7] + m)
                for t in range(TT):
                    last = pe.transpose(bank[7][:, t * P:(t + 1) * P], x1T[:, m, t * P:(t + 1) * P], ident[:, :])
                last.then_inc(x1_turned, 1)

            for m in range(KD):
                pe.wait_ge(x_cols_in[m % 4], 16 * (m // 4 + 1))
                free(6, used_out[6] + m)
                for t in range(TT):
                    last = pe.transpose(bank[6][:, t * P:(t + 1) * P], x_cols[m % 4][:, t, :], ident[:, :])
                last.then_inc(x_turned, 1)
                pe.wait_ge(lo_split, OUT0 + m + 1)
                free(m % 2, used_out[m % 2] + m // 2)
                project(slots[OUT0 + m], bank[m % 2][:, :], mrg_hi, mrg_lo, KD,
                        tiles_ready=merged_ready if m == 0 else None, before=1).then_inc(blocks_done, 1)
                if m:
                    turn_back(m - 1)
            turn_back(KD - 1)

            uses = list(used_ffn)
            for half in range(2):
                n0 = FFN0 + half * FFN_HALF_BLOCKS
                pair = FF1_BANKS[half]
                with pe.Fori(0, HALF // 4) as q:
                    for jj in range(4):
                        b = pair[jj % 2]
                        pe.wait_ge(lo_split, 4 * q + n0 + jj + 1)
                        pe.wait_ge(bank_free[b], 2 * q + uses[b] + jj // 2)
                        project(slots[n0 + jj], bank[b][:, :], h2_hi, h2_lo, KD,
                                tiles_ready=h2_ready if half == jj == 0 else None).then_inc(blocks_done, 1)
                for b in pair:
                    uses[b] += HALF // 2
                if half == 0:
                    pe.wait_ge(sumsq_set, KD - 1)
                    free(6, used_out[6] + KD)
                    for t in range(TT):
                        last = pe.matmul(bank[6][:, t:t + 1], sumsq[:, t * P:(t + 1) * P], mean_col[:, 0:1],
                                         start=True, stop=True)
                    last.then_inc(ms_done, 1)
                for f in range(2):
                    four = FF2_BANKS[half][f]
                    for b in four:
                        free(b, uses[b])
                        uses[b] += 1
                    def add_block(g, t):
                        s, tok = slots[n0 + HALF + f * GROUP + g], slice(t * P, (t + 1) * P)
                        for kk in range(2):
                            k, c = 2 * g + kk, slice(kk * S, (kk + 1) * S)
                            last = three(bank[four[t]][:, :], hid_hi[:, k, tok], hid_lo[:, k, tok],
                                         w_hi[s][:, c], w_lo[s][:, c], k == 0, k == HALF - 1)
                        return last

                    by_tokens = 2 if half == f == 1 else 0
                    for g in range(GROUP - by_tokens):
                        pe.wait_ge(lo_split, n0 + HALF + f * GROUP + g + 1)
                        pe.wait_ge(hid_ready, half * HALF + 2 * g + 2)
                        for t in range(TT):
                            last = add_block(g, t)
                        last.then_inc(blocks_done, 1)
                    if by_tokens:
                        pe.wait_ge(lo_split, BLOCKS)
                        for t in range(TT):
                            for g in range(GROUP - by_tokens, GROUP):
                                last = add_block(g, t)
                            last.then_inc(tokens_done, 1)

        @block.scalar
        def _(act):
            act.preload_act_table(ACT.Exp)

            rounds = Tally()

            def split(n, per=0, i=0):
                s = slots[n]
                act.wait_ge(raw_in[s], 32 * i + 32 if s == RING - 1 else 16 * i + 16 * loads[n])
                if n >= DEPTH:
                    act.wait_ge(blocks_done, per * i + n - DEPTH + 1)
                act.activation(w_hi[s][:, :], w_raw[s][:, :], ACT.Copy).then_inc(hi_split, 1)

            def round_to(dst, src, scale=1.0):
                act.activation(dst, src, ACT.Copy, scale=scale).then_inc(hi_written, 1)

            def square_rows(s):
                act.wait_ge(stage_in[s], 16)
                if s:
                    act.wait_ge(squares_summed, s)
                act.activation(square_junk[:, :], stage[s][:, :], ACT.Square,
                               accum_out=ssq[:, s:s + 1]).then_inc(squares_summed, 1)

            def turn_back_head(i, banks):
                for c, (b, uses) in enumerate(banks):
                    act.wait_ge(bank_free[b], uses + 1)
                    round_to(ret_hi[:, 2 * i + c, :], (work_a, work_c)[c][:, :])

            def copy_gain(g, c):
                act.wait_ge(gains_spread, 2 * g + c + 1)
                act.activation((gain_mem, gain_x)[g][:, c * S:(c + 1) * S], bank[4 * g + c][:, :], ACT.Copy)\
                    .then_inc(gains_copied, 1)

            copy_gain(0, 0)
            square_rows(0)
            copy_gain(0, 1)
            square_rows(1)
            for kind, i, n, banks in STEPS:
                if (kind, i) == LAST_TURN:
                    continue
                b = banks[0][0] if banks else None
                if kind in BLOCK_STEPS:
                    for more in range(2 if kind == "v" else 1):
                        split(n + AHEAD + more)
                if kind == "turn":
                    hi = memT_hi if i < MT else h_hi
                    tok = slice((i % MT) * P, (i % MT + 1) * P) if i < MT else slice((i - MT) * P, (i - MT + 1) * P)
                    for c, (b, _) in enumerate(banks):
                        act.wait_ge(turned, 2 * i + c + 1)
                        round_to(hi[:, 4 * c:4 * c + 4, tok], bank[b][:, :].rearrange("p (k n) -> p k n", n=P))
                    if i < AHEAD:
                        split(i)
                    if i == MT - 1:
                        copy_gain(1, 0)
                        copy_gain(1, 1)
                elif kind == "mem_k":
                    act.wait_ge(blocks_done, n + 1)
                    round_to(memK_hi[:, i, :], bank[b][:, 0:M])
                    square_rows(MT + i)
                elif kind == "mem_v" and i == 3:
                    act.wait_ge(blocks_done, n + 1)
                    for t in range(MT):
                        round_to(memV_hi[:, t, :], bank[banks[t][0]][:, :])
                elif kind == "mem_q":
                    if i == 0:
                        act.wait_ge(logit_abs, 1)
                        act.activation(exp_abs[:, :], lg_work[:, :], ACT.Exp).then_inc(logit_exp, 1)
                        act.activation(grp_hi[:, :, :], grp_raw[:, :, :], ACT.Copy).then_inc(grp_rounded, 1)
                    act.wait_ge(blocks_done, n + 1)
                    round_to(mq_hi[:, i, :], bank[b][:, :])
                elif kind == "pool":
                    act.wait_ge(pads_set, 2)
                    act.wait_ge(blocks_done, n + 1)
                    if i >= 2:
                        act.wait_ge(mixed, i - 1)
                    act.activation(padded[i % 2][:, PAD:PAD + S], bank[b][:, :], ACT.Copy)\
                        .then_inc(bank_free[b], 1)
                elif kind == "mean":
                    act.wait_ge(to_round, rounds.next())
                    if i >= 2:
                        act.wait_ge(mix_done, i - 1)
                    round_to(mix_hi[i % 2][:, :], work_a[:, :])
                elif kind == "mix":
                    act.wait_ge(mix_done, i + 1)
                    round_to(pool_hi[:, i, :], bank[b][:, :], pscale[:, i:i + 1])
                elif kind == "att_s":
                    act.wait_ge(max_set, i + 1)
                    for t in range(TT):
                        e = act.activation(probs[:, t, :], bank[banks[t // 2][0]][:, (t % 2) * M:(t % 2 + 1) * M],
                                           ACT.Exp, bias=row_max[:, t:t + 1], scale=QK_SCALE,
                                           accum_out=row_sum[:, t:t + 1])
                        if t % 2:
                            e.then_inc(bank_free[banks[t // 2][0]], 1)
                elif kind == "att_t":
                    act.wait_ge(probs_turned, i + 1)
                    for c in range(MT):
                        round_to(probT_hi[:, c, :], bank[banks[c][0]][:, :])
                elif kind == "att_o":
                    act.wait_ge(att_done, i + 1)
                    round_to(att_hi[:, i, :], bank[b][:, :])
                elif kind in ("q", "k"):
                    act.wait_ge(blocks_done, n + 1)
                    turn = 2 * i + (kind == "k")
                    if turn:
                        act.wait_ge(sin_done, turn)
                    half = P // 2
                    act.activation(swapped[0:half, :], bank[b][half:P, :], ACT.Copy)
                    act.activation(swapped[half:P, :], bank[b][0:half, :], ACT.Copy).then_inc(halves_swapped, 1)
                    act.wait_ge(to_round, rounds.next())
                    round_to(qk_hi[:, int(kind == "k"), :], work_a[:, :])
                elif kind == "v":
                    act.wait_ge(log_decay_set, i + 1)
                    act.activation(decay[:, :], decay_a[:, :], ACT.Exp).then_inc(decay_set, 1)
                    act.wait_ge(blocks_done, n + 2)
                    for c, (b, _) in enumerate(banks):
                        round_to(v_hi[:, 2 * c:2 * c + 2, :], bank[b][:, :].rearrange("p (t e) -> p t e", e=VD))
                elif kind == "g":
                    act.wait_ge(blocks_done, n + 1)
                    if i:
                        b0, uses = banks_of["g", i - 1][0]
                        act.wait_ge(bank_free[b0], uses + 1)
                    act.activation(sig_g[:, :], bank[b][:, :], ACT.Sigmoid).then_inc(sigmoid_g, 1)
                elif kind == "ret_s":
                    for jj, (b, uses) in enumerate(banks):
                        act.wait_ge(bank_free[b], uses + 1)
                        round_to(s_hi[:, 2 * (i % 2) + jj, :], (work_a, work_c)[jj][:, :])
                elif kind == "ret_t":
                    turn_back_head(i, banks)

            act.preload_act_table(ACT.Sigmoid)
            def merge_tile(m, first=False):
                for g in range(N_BRANCHES):
                    split(MERGE0 + AHEAD + g, 5, m)
                    act.wait_ge(blocks_done, 5 * m + MERGE0 + g + 1)
                    if g == 0:
                        act.wait_ge(merged_ready, m + 1)
                    act.activation(sig[g][:, :], bank[g][:, :], ACT.Sigmoid).then_inc(bank_free[g], 1)
                    if first and g == 0:
                        turn_back_head(HEADS - 1, banks_of[LAST_TURN])
                split(MERGE0 + AHEAD + 3, 5, m)
                split(MERGE0 + AHEAD + 4, 5, m)
                act.wait_ge(to_round, m + rounds.n + 1)
                round_to(mrg_hi[:, bass.ds(m, 1), :], sig[0][:, :].rearrange("p (a s) -> p a s", a=1))

            merge_tile(0, first=True)
            with act.Fori(1, KD) as m:
                merge_tile(m)
            rounds.n += KD

            act.wait_ge(blocks_done, OUT0)

            def back(m):
                act.wait_ge(x1_turned, m + 1)
                act.activation(x1[:, :, m * P:(m + 1) * P], bank[7][:, :].rearrange("p (t n) -> p t n", n=P),
                               ACT.Copy).then_inc(bank_free[7], 1)

            for m in range(KD):
                split(OUT0 + m + AHEAD)
                act.wait_ge(x_turned, m + 1)
                act.activation(x1T[:, m, :], bank[6][:, :], ACT.Copy).then_inc(bank_free[6], 1)
                if m:
                    back(m - 1)
                act.wait_ge(bank_free[m % 2], used_out[m % 2] + m // 2 + 1)
                if m >= 3:
                    act.wait_ge(sumsq_set, m - 2)
                act.activation((square[m % 2] if m else sumsq)[:, :], x1T[:, m, :], ACT.Square).then_inc(square_set, 1)
                round_to(h2_hi[:, m, :], x1T[:, m, :], gain2[:, m:m + 1])
            back(KD - 1)

            act.wait_ge(sumsq_set, KD - 1)
            for half in range(2):
                n0 = FFN0 + half * FFN_HALF_BLOCKS
                pair = FF1_BANKS[half]
                with act.Fori(0, HALF // 4) as q:
                    for jj in range(4):
                        b = pair[jj % 2]
                        split(n0 + jj + AHEAD, 4, q)
                        act.wait_ge(blocks_done, 4 * q + n0 + jj + 1)
                        act.activation(relu[jj % 2][:, :], bank[b][:, :], ACT.Relu).then_inc(bank_free[b], 1)
                        act.wait_ge(to_round, 4 * q + rounds.n + jj + 1)
                        round_to(hid_hi[:, bass.ds(4 * q + jj, 1), :],
                                 relu2[jj % 2][:, :].rearrange("p (a s) -> p a s", a=1))
                rounds.n += HALF
                for f in range(2):
                    for g in range(GROUP):
                        n = n0 + HALF + f * GROUP + g
                        if n + AHEAD < BLOCKS:
                            split(n + AHEAD)
                    if half == 1:
                        for t in range(TT):
                            b = FF2_BANKS[half][f][t]
                            act.wait_ge(bank_free[b], ffn_uses[half][f][t] + 1)
                            if 4 * f + t:
                                act.wait_ge(half_sums, 4 * f + t)
                            act.activation(relu[t % 2][:, :], x1[:, t, f * S:(f + 1) * S], ACT.Square,
                                           accum_out=ssq[:, 4 * f + t:4 * f + t + 1]).then_inc(half_sums, 1)
                            if f == 1:
                                act.wait_ge(rms_set, MT + TT + t + 1)
                                act.activation(y[t][:, 0:S], x2g[:, t, :], ACT.Copy, scale=rms[:, t:t + 1])\
                                    .then_inc(y_ready[0], 1)

        @block.vector
        def _(dve):
            rounded, steps = Tally(), Tally()

            def link(ins):
                ins.then_inc(vec_step, 1)
                dve.wait_ge(vec_step, steps.next())

            def past(counter, value):
                if value > 0:
                    dve.wait_ge(counter, value)

            def split(n, per=0, i=0):
                s = slots[n]
                dve.wait_ge(hi_split, per * i + n + 1)
                dve.tensor_tensor(w_lo[s][:, :], w_raw[s][:, :], r32(w_hi[s][:, :]), ALU.subtract)\
                    .then_inc(lo_split, 1)

            def rest(dst, src, hi, scale=None):
                dve.wait_ge(hi_written, rounded.next())
                if scale is None:
                    return dve.tensor_tensor(dst, src, r32(hi), ALU.subtract)
                return dve.scalar_tensor_tensor(out=dst, in0=src, scalar=scale, in1=r32(hi),
                                                op0=ALU.mult, op1=ALU.subtract)

            def norm_rows(s, gain):
                dve.wait_ge(squares_summed, s + 1)
                dve.tensor_scalar(msq[:, s:s + 1], ssq[:, s:s + 1], 1.0 / D, EPS, ALU.mult, ALU.add)\
                    .then_inc(msq_set, 1)
                dve.wait_ge(rms_set, s + 1)
                dve.scalar_tensor_tensor(out=stage[s][:, :], in0=stage[s][:, :], scalar=rms[:, s:s + 1],
                                         in1=gain[:, :], op0=ALU.mult, op1=ALU.mult).then_inc(normed, 1)

            def log_sigmoid():
                dve.wait_ge(late_in, LATE)
                link(dve.tensor_scalar(lg_work[:, :], logit[:, :], -1.0, None, ALU.mult))
                dve.tensor_tensor(lg_work[:, :], lg_work[:, :], logit[:, :], ALU.min).then_inc(logit_abs, 1)
                dve.wait_ge(logit_exp, 1)
                link(dve.tensor_scalar(lg_z[:, :], exp_abs[:, :], 2.0, None, ALU.add))
                link(dve.reciprocal(lg_z[:, :], lg_z[:, :]))
                link(dve.tensor_tensor(lg_z[:, :], lg_z[:, :], exp_abs[:, :], ALU.mult))
                link(dve.tensor_tensor(lg_z2[:, :], lg_z[:, :], lg_z[:, :], ALU.mult))
                link(dve.tensor_scalar(log_g[:, :], lg_z2[:, :], 1.0 / 17, None, ALU.mult))
                for odd in range(15, 0, -2):
                    link(dve.scalar_tensor_tensor(out=log_g[:, :], in0=log_g[:, :], scalar=1.0 / odd,
                                                  in1=(lg_z2 if odd > 1 else lg_z)[:, :],
                                                  op0=ALU.add, op1=ALU.mult))
                link(dve.tensor_scalar(lg_work[:, :], logit[:, :], 0.0, None, ALU.min))
                link(dve.scalar_tensor_tensor(out=log_g[:, :], in0=log_g[:, :], scalar=-2.0,
                                              in1=lg_work[:, :], op0=ALU.mult, op1=ALU.add))

            def window_means(i):
                dve.wait_ge(sums_done, i + 1)
                past(mixed, i)
                link(dve.tensor_tensor(work_a[:, :], sums[i % 2][:, PAD:PAD + S], counts[:, i, :], ALU.mult))
                dve.tensor_tensor(work_a[:, :], work_a[:, :], padded[i % 2][:, PAD:PAD + S], ALU.subtract)\
                    .then_inc(to_round, 1)
                rest(mix_lo[i % 2][:, :], work_a[:, :], mix_hi[i % 2][:, :]).then_inc(mixed, 1)

            def turn_back_head(i, banks):
                b0, uses = banks_of["g", 2 * i + 1][0]
                dve.wait_ge(bank_free[b0], uses + 1)
                for c, (b, _) in enumerate(banks):
                    dve.wait_ge(ret_turned, 2 * i + c + 1)
                    past(s_ready, 4 * i + 4)
                    past(qk_ready, min(2 * i + 4, 2 * HEADS))
                    dve.tensor_tensor((work_a, work_c)[c][:, :], bank[b][:, :], gate_g[:, c, :], ALU.mult)\
                        .then_inc(bank_free[b], 1)
                for c in range(2):
                    rest(ret_lo[:, 2 * i + c, :], (work_a, work_c)[c][:, :], ret_hi[:, 2 * i + c, :])\
                        .then_inc(ret_ready, 1)

            dve.wait_ge(gains_copied, 2)
            norm_rows(0, gain_mem)
            norm_rows(1, gain_mem)
            for kind, i, n, banks in STEPS:
                if (kind, i) == LAST_TURN:
                    continue
                b = banks[0][0] if banks else None
                if kind in BLOCK_STEPS:
                    for more in range(2 if kind == "v" else 1):
                        split(n + AHEAD + more)
                if kind == "turn":
                    hi, lo = (memT_hi, memT_lo) if i < MT else (h_hi, h_lo)
                    tok = slice(i * P, (i + 1) * P) if i < MT else slice((i - MT) * P, (i - MT + 1) * P)
                    for c, (b, _) in enumerate(banks):
                        rest(lo[:, 4 * c:4 * c + 4, tok], bank[b][:, :].rearrange("p (k n) -> p k n", n=P),
                             hi[:, 4 * c:4 * c + 4, tok]).then_inc(bank_free[b], 1)
                    if i < AHEAD:
                        split(i)
                elif kind == "mem_k":
                    rest(memK_lo[:, i, :], bank[b][:, 0:M], memK_hi[:, i, :]).then_inc(bank_free[b], 1)
                    if i == 0:
                        dve.wait_ge(gains_copied, 4)
                    norm_rows(MT + i, gain_x)
                elif kind == "mem_v" and i == 3:
                    for t in range(MT):
                        b = banks[t][0]
                        rest(memV_lo[:, t, :], bank[b][:, :], memV_hi[:, t, :]).then_inc(bank_free[b], 1)
                elif kind == "mem_q":
                    if i == 0:
                        log_sigmoid()
                        dve.wait_ge(grp_rounded, 1)
                        dve.tensor_tensor(grp_lo[:, :, :], grp_raw[:, :, :], r32(grp_hi[:, :, :]), ALU.subtract)\
                            .then_inc(grp_split, 1)
                    rest(mq_lo[:, i, :], bank[b][:, :], mq_hi[:, i, :]).then_inc(bank_free[b], 1)
                elif kind == "mean":
                    window_means(i)
                elif kind == "mix":
                    rest(pool_lo[:, i, :], bank[b][:, :], pool_hi[:, i, :], pscale[:, i:i + 1]).then_inc(bank_free[b], 1)
                elif kind == "att_s":
                    dve.wait_ge(scores_done, i + 1)
                    for c, (b, _) in enumerate(banks):
                        link(dve.tensor_reduce(row_max[:, 2 * c:2 * c + 2],
                                               bank[b][:, :].rearrange("p (t m) -> p t m", m=M), AX.X, ALU.max))
                    dve.tensor_scalar(row_max[:, 0:4], row_max[:, 0:4], -QK_SCALE, None, ALU.mult).then_inc(max_set, 1)
                    for b, uses in banks:
                        dve.wait_ge(bank_free[b], uses + 1)
                    link(dve.reciprocal(row_inv[:, 0:4], row_sum[:, 0:4]))
                    for t in range(TT):
                        ins = dve.tensor_scalar(probs[:, t, :], probs[:, t, :], row_inv[:, t:t + 1], None, ALU.mult)
                    ins.then_inc(probs_set, 1)
                elif kind == "att_t":
                    for c, (b, _) in enumerate(banks):
                        rest(probT_lo[:, c, :], bank[b][:, :], probT_hi[:, c, :]).then_inc(bank_free[b], 1)
                elif kind == "att_o":
                    rest(att_lo[:, i, :], bank[b][:, :], att_hi[:, i, :]).then_inc(bank_free[b], 1)
                elif kind in ("q", "k"):
                    turn = 2 * i + (kind == "k")
                    dve.wait_ge(halves_swapped, turn + 1)
                    past(mixed, 4)
                    past(qk_ready, turn)
                    past(s_ready, 4 * i)
                    past(ret_ready, 2 * i - 2)
                    dve.tensor_tensor(work_a[:, :], bank[b][:, :], cos[:, :], ALU.mult).then_inc(bank_free[b], 1)
                    dve.wait_ge(bank_free[b], banks[0][1] + 1)
                    dve.wait_ge(sin_done, turn + 1)
                    dve.tensor_tensor(work_a[:, :], work_a[:, :], work_b[:, :], ALU.add).then_inc(to_round, 1)
                    c = int(kind == "k")
                    rest(qk_lo[:, c, :], work_a[:, :], qk_hi[:, c, :]).then_inc(qk_ready, 1)
                elif kind == "v":
                    if i:
                        dve.wait_ge(ret_values_done, i)
                    dve.tensor_scalar(decay_a[:, :], dist[:, :], 0.0, log_g[:, i:i + 1], ALU.max, ALU.mult)
                    link(dve.tensor_scalar(decay_b[:, :], dist[:, :], 0.0, log_g[:, 4 + i:5 + i],
                                           ALU.min, ALU.mult))
                    dve.tensor_tensor(decay_a[:, :], decay_a[:, :], decay_b[:, :], ALU.subtract)\
                        .then_inc(log_decay_set, 1)
                    for c, (b, _) in enumerate(banks):
                        rest(v_lo[:, 2 * c:2 * c + 2, :], bank[b][:, :].rearrange("p (t e) -> p t e", e=VD),
                             v_hi[:, 2 * c:2 * c + 2, :]).then_inc(bank_free[b], 1)
                elif kind == "g":
                    dve.wait_ge(sigmoid_g, i + 1)
                    dve.tensor_tensor(gate_g[:, i % 2, :], sig_g[:, :], bank[b][:, :], ALU.mult)\
                        .then_inc(bank_free[b], 1)
                elif kind == "ret_s":
                    dve.wait_ge(decay_set, i // 2 + 1)
                    for jj, (b, _) in enumerate(banks):
                        j = 2 * (i % 2) + jj
                        dve.wait_ge(ret_scores_done, 2 * i + jj + 1)
                        past(s_ready, 2 * i)
                        past(qk_ready, 2 * (i // 2) + 2)
                        past(ret_ready, 2 * (i // 2))
                        dve.scalar_tensor_tensor(out=(work_a, work_c)[jj][:, :], in0=bank[b][:, :],
                                                 scalar=QK_SCALE, in1=decay[:, REACH - j * P:REACH - j * P + S],
                                                 op0=ALU.mult, op1=ALU.mult).then_inc(bank_free[b], 1)
                    for jj in range(2):
                        j = 2 * (i % 2) + jj
                        rest(s_lo[:, j, :], (work_a, work_c)[jj][:, :], s_hi[:, j, :]).then_inc(s_ready, 1)
                elif kind == "ret_v":
                    dve.wait_ge(ret_values_done, i + 1)
                    for t in range(TT):
                        ins = dve.bn_stats(stats[:, 6 * t:6 * t + 6],
                                           bank[banks[t // 2][0]][:, (t % 2) * VD:(t % 2 + 1) * VD])
                    link(ins)
                    for t in range(TT):
                        ins = dve.bn_aggr(moments[:, 2 * t:2 * t + 2], stats[:, 6 * t:6 * t + 6])
                    link(ins)
                    dve.tensor_scalar(ret_var[:, 0:4], moments[:, 1:8:2], EPS, None, ALU.add).then_inc(var_set, 1)
                    dve.wait_ge(rstd_set, i + 1)
                    for t in range(TT):
                        b = banks[t // 2][0]
                        ins = dve.tensor_scalar(o_nat[:, t, :], bank[b][:, (t % 2) * VD:(t % 2 + 1) * VD],
                                                moments[:, 2 * t:2 * t + 1], ret_rstd[:, t:t + 1],
                                                ALU.subtract, ALU.mult)
                        if t % 2:
                            ins.then_inc(bank_free[b], 1)
                elif kind == "ret_t":
                    turn_back_head(i, banks)

            chain0 = steps.n
            dve.sem_inc(merged_ready, 1)
            def merge_tile(m, hi_before, first=False):
                if first:
                    split(MERGE0 + AHEAD)
                    turn_back_head(HEADS - 1, banks_of[LAST_TURN])
                for g in range(1 if first else 0, 4):
                    split(MERGE0 + AHEAD + g, 5, m)
                for g in range(N_BRANCHES):
                    if g < 2:
                        dve.wait_ge(blocks_done, 5 * m + MERGE0 + 4 + g)
                    dve.wait_ge(bank_free[g], m + used_merge[g] + 1)
                    dve.tensor_tensor(sig[g][:, :], sig[g][:, :], bank[3 + g][:, :], ALU.mult)\
                        .then_inc(bank_free[3 + g], 1)
                split(MERGE0 + AHEAD + 4, 5, m)
                for g in (0, 1):
                    dve.wait_ge(bank_free[3 + g], m + used_merge[3 + g] + 1)
                dve.tensor_tensor(sig[0][:, :], sig[0][:, :], sig[1][:, :], ALU.add).then_inc(vec_step, 1)
                dve.wait_ge(vec_step, m + chain0 + 1)
                dve.wait_ge(bank_free[5], m + used_merge[5] + 1)
                dve.tensor_tensor(sig[0][:, :], sig[0][:, :], sig[2][:, :], ALU.add).then_inc(to_round, 1)
                dve.wait_ge(hi_written, m + hi_before + 1)
                dve.tensor_tensor(mrg_lo[:, bass.ds(m, 1), :], sig[0][:, :].rearrange("p (a s) -> p a s", a=1),
                                  r32(mrg_hi[:, bass.ds(m, 1), :]), ALU.subtract).then_inc(merged_ready, 1)

            merge_tile(0, rounded.n + 2, first=True)
            with dve.Fori(1, KD) as m:
                merge_tile(m, rounded.n)
            steps.n += KD
            rounded.n += KD

            for m in range(KD):
                split(OUT0 + m + AHEAD)
                dve.wait_ge(bank_free[6], used_out[6] + m + 1)
                dve.wait_ge(blocks_done, OUT0 + m + 1)
                dve.tensor_tensor(x1T[:, m, :], bank[m % 2][:, :], x1T[:, m, :], ALU.add)\
                    .then_inc(bank_free[m % 2], 1)
                rest(h2_lo[:, m, :], x1T[:, m, :], h2_hi[:, m, :], gain2[:, m:m + 1]).then_inc(h2_ready, 1)

            for half in range(2):
                n0 = FFN0 + half * FFN_HALF_BLOCKS
                pair = FF1_BANKS[half]
                with dve.Fori(0, HALF // 4) as q:
                    for jj in range(4):
                        b = pair[jj % 2]
                        split(n0 + jj + AHEAD, 4, q)
                        dve.wait_ge(bank_free[b], 2 * q + ff1_uses[half][jj % 2] + jj // 2 + 1)
                        dve.tensor_tensor(relu2[jj % 2][:, :], relu[jj % 2][:, :], relu[jj % 2][:, :], ALU.mult)\
                            .then_inc(to_round, 1)
                        dve.wait_ge(hi_written, 4 * q + rounded.n + jj + 1)
                        dve.tensor_tensor(hid_lo[:, bass.ds(4 * q + jj, 1), :],
                                          relu2[jj % 2][:, :].rearrange("p (a s) -> p a s", a=1),
                                          r32(hid_hi[:, bass.ds(4 * q + jj, 1), :]), ALU.subtract)\
                            .then_inc(hid_ready, 1)
                rounded.n += HALF
                if half == 0:
                    dve.wait_ge(ms_done, 1)
                    dve.tensor_scalar(msq[:, 0:4], bank[6][:, 0:4], EPS, None, ALU.add).then_inc(bank_free[6], 1)
                    dve.wait_ge(bank_free[6], used_out[6] + KD + 1)
                    link(dve.reciprocal(inv_ms[:, 0:4], msq[:, 0:4]))
                    dve.wait_ge(bank_free[7], used_out[7] + KD)
                for f in range(2):
                    four, uses = FF2_BANKS[half][f], ffn_uses[half][f]
                    for g in range(GROUP):
                        n = n0 + HALF + f * GROUP + g
                        if n + AHEAD < BLOCKS:
                            split(n + AHEAD)
                        if half == f == 1 and g < TT:
                            if g == 0:
                                dve.wait_ge(gain_in, 16)
                            dve.wait_ge(half_sums, g + 1)
                            dve.tensor_tensor(x2g[:, g, :], x1[:, g, 0:S], gain_f[:, 0:S], ALU.mult)
                        if half == f == 1 and g == TT:
                            link(dve.tensor_scalar(half_mean[:, 0:4], ssq[:, 0:4], 1.0 / D, EPS, ALU.mult, ALU.add))
                    if half == 0 or f == 0:
                        dve.wait_ge(blocks_done, n0 + HALF + (f + 1) * GROUP)
                    for t in range(TT):
                        if half == f == 1:
                            dve.wait_ge(tokens_done, t + 1)
                        if half:
                            dve.wait_ge(bank_free[FF2_BANKS[0][f][t]], ffn_uses[0][f][t] + 1)
                        part = x1[:, t, f * S:(f + 1) * S]
                        dve.scalar_tensor_tensor(out=part, in0=bank[four[t]][:, :], scalar=inv_ms[:, t:t + 1],
                                                 in1=part, op0=ALU.mult, op1=ALU.add).then_inc(bank_free[four[t]], 1)
                        if half == f == 1:
                            dve.wait_ge(half_sums, TT + t + 1)
                            dve.scalar_tensor_tensor(out=msq[:, t:t + 1], in0=ssq[:, 4 + t:5 + t], scalar=1.0 / D,
                                                     in1=half_mean[:, t:t + 1], op0=ALU.mult, op1=ALU.add)\
                                .then_inc(msq_set, 1)
                            dve.wait_ge(rms_set, MT + TT + t + 1)
                            dve.scalar_tensor_tensor(out=y[t][:, S:D], in0=part, scalar=rms[:, t:t + 1],
                                                     in1=gain_f[:, S:D], op0=ALU.mult, op1=ALU.mult)\
                                .then_inc(y_ready[1], 1)

        @block.gpsimd
        def _(pool):
            pool.memset(minus_half[:, :], -0.5).then_inc(consts_set, 1)
            pool.memset(mean_col[:, :], 1.0 / D).then_inc(consts_set, 1)
            pool.memset(ones_row[:, :], 1.0).then_inc(consts_set, 1)
            pool.wait_ge(consts_set, 3)

            def inv_sqrt(dst, src, width):
                return pool.tensor_tensor(dst, src, minus_half[:, 0:width], ALU.pow)

            for s in range(MT + TT):
                pool.wait_ge(msq_set, s + 1)
                inv_sqrt(rms[:, s:s + 1], msq[:, s:s + 1], 1).then_inc(rms_set, 1)
            for b, uses in banks_of["turn", MT + 2] + banks_of["turn", MT + 3]:
                pool.wait_ge(bank_free[b], uses + 1)
            for p in padded:
                pool.memset(p[:, :], 0.0).then_inc(pads_set, 1)

            added = 0

            for kind, i, n, banks in STEPS:
                if kind in ("q", "k"):
                    turn = 2 * i + (kind == "k")
                    pool.wait_ge(halves_swapped, turn + 1)
                    if turn:
                        pool.wait_ge(qk_ready, turn)
                    pool.tensor_tensor(work_b[:, :], swapped[:, :], sin[:, :], ALU.mult).then_inc(sin_done, 1)
                elif kind == "pool":
                    b, uses = banks[0]
                    pool.wait_ge(bank_free[b], uses + 1)
                    if i:
                        pool.wait_ge(mixed, i)
                    width = S + 2 * PAD
                    p, dst, src = padded[i % 2], sums[0], sums[1]
                    ins = pool.tensor_tensor(dst[:, 1:width], p[:, 1:width], p[:, 0:width - 1], ALU.add)
                    lo, hi, reach = 1, width, 1
                    for _ in range(i):
                        ins.then_inc(pool_step, 1)
                        added += 1
                        pool.wait_ge(pool_step, added)
                        src, dst = dst, src
                        lo, hi = lo + reach, hi - reach
                        ins = pool.tensor_tensor(dst[:, lo:hi], src[:, lo + reach:hi + reach],
                                                 src[:, lo - reach:hi - reach], ALU.add)
                        reach *= 2
                    ins.then_inc(sums_done, 1)
                elif kind == "ret_v":
                    pool.wait_ge(var_set, i + 1)
                    inv_sqrt(ret_rstd[:, 0:4], ret_var[:, 0:4], 4).then_inc(rstd_set, 1)

            for m in range(1, KD):
                pool.wait_ge(square_set, m + 1)
                if m > 1:
                    pool.wait_ge(sumsq_set, m - 1)
                pool.tensor_tensor(sumsq[:, :], sumsq[:, :], square[m % 2][:, :], ALU.add).then_inc(sumsq_set, 1)

            for t in range(TT):
                pool.wait_ge(msq_set, MT + TT + t + 1)
                inv_sqrt(rms[:, t:t + 1], msq[:, t:t + 1], 1).then_inc(rms_set, 1)


_INS = ["x", "mem", "w_in", "ret_decay_logit", "w_ret_o", "w_pool_grp", "pool_scale", "w_pool_o",
        "w_mem_kv", "w_mem_o", "w_out", "w_ff1", "w_ff2", "norm1_g", "norm2_g", "mem_norm_g",
        "final_norm_g"]


def shape_tables():
    f32 = np.float32
    inv = (f32(10000.0) ** (-np.arange(0, P, 2, dtype=f32) / f32(P))).astype(f32)
    angle = (np.arange(S, dtype=f32)[None, :] * inv[:, None]).astype(f32)
    cos, sin = np.cos(angle).astype(f32), np.sin(angle).astype(f32)
    distance = np.arange(SPAN)[None, :] - np.arange(P)[:, None] - REACH
    n = np.arange(S)
    counts = [1.0 / (np.clip(n + w // 2, 0, S) - np.clip(n - w // 2, 0, S)) for w in POOL_WINDOWS]
    return {
        "identity": np.eye(P, dtype=f32),
        "cos_table": np.concatenate([cos, cos]),
        "sin_table": np.concatenate([-sin, sin]),
        "distance": distance.astype(f32),
        "inv_count": np.concatenate(counts)[None, :].astype(f32),
    }


def kernel(**inputs):
    import concourse.bacc as bacc
    from concourse.bass_utils import run_bass_kernel_spmd

    nc = bacc.Bacc("TRN2", target_bir_lowering=False, num_devices=1)
    arrays, args = {}, []
    given = {name: np.ascontiguousarray(inputs[name]) for name in _INS}
    for name, a in {**given, **shape_tables()}.items():
        arrays[f"in_{name}"] = a
        args.append(nc.dram_tensor(f"in_{name}", a.shape, mybir.dt.from_np(a.dtype), kind="ExternalInput").ap())
    out = nc.dram_tensor("out", (1, S, D), FP32, kind="ExternalOutput").ap()
    encoder_kernel(nc, *args, out)
    result = run_bass_kernel_spmd(nc, [arrays], core_ids=[0])
    return result.results[0]["out"]
```

```python
from contextlib import ExitStack

import numpy as np
import concourse.bass as bass
from concourse import mybir

FP32 = mybir.dt.float32
FP32R = mybir.dt.float32r
ALU = mybir.AluOpType
ACT = mybir.ActivationFunctionType
AX = mybir.AxisListType

P = 128
D = 1024
S = 512
KD = D // P
TT = S // P
M = 256
MT = M // P
HEADS = 4
VD = 256
POOL_WINDOWS = (2, 4, 8, 16)
PAD = max(POOL_WINDOWS) // 2
HIDDEN = 4 * D
N_BRANCHES = 3
EPS = 1e-6
QK_SCALE = float(P) ** -0.5
BLOCK = 1024
RING = 5
DEPTH = 4
AHEAD = 3
KB = 1024

COL_Q, COL_K, COL_V, COL_G = 0, 512, 1024, 2048
COL_POOL, COL_MQ, COL_GATES = 3072, 3584, 4096

REACH = S - P
SPAN = REACH + S


def projection_steps():
    order = [("turn", 0), ("turn", 1)]
    order += [("mem_v", b) for b in range(3)]
    order += [("turn", MT), ("mem_v", 3)]
    for h in range(3):
        order += [("turn", MT + 1 + h), ("mem_k", h)]
    order.append(("mem_k", 3))
    order += [("mem_q", 0), ("mem_q", 1), ("att_s", 0), ("mem_q", 2), ("att_t", 0),
              ("mem_q", 3), ("att_o", 0),
              ("pool", 0), ("att_s", 1), ("pool", 1), ("mean", 0), ("att_t", 1),
              ("pool", 2), ("mean", 1), ("mix", 0), ("att_o", 1),
              ("pool", 3), ("mean", 2), ("mix", 1), ("att_s", 2), ("mean", 3)]
    more = {("q", 0): [("mix", 2), ("att_t", 2)], ("k", 0): [("mix", 3)],
            ("v", 0): [("att_o", 2)], ("ret_s", 1): [("att_s", 3)], ("ret_v", 0): [("att_t", 3)],
            ("q", 1): [("att_o", 3)]}
    for h in range(HEADS):
        for step in (("q", h), ("k", h), ("v", h), ("g", 2 * h), ("g", 2 * h + 1)):
            order += [step] + more.get(step, [])
            if step[0] == "k" and h > 0:
                order.append(("ret_t", h - 1))
            if step[0] == "v":
                order += [("ret_s", 2 * h)] + more.get(("ret_s", 2 * h), [])
            if step == ("g", 2 * h):
                order += [("ret_s", 2 * h + 1)] + more.get(("ret_s", 2 * h + 1), [])
            if step == ("g", 2 * h + 1):
                order += [("ret_v", h)] + more.get(("ret_v", h), [])
    order.append(LAST_TURN)

    fixed = {"mem_v": (4, 5), "v": (4, 5), "att_s": (6, 7), "att_t": (6, 7), "att_o": (2,),
             "ret_s": (2, 3), "ret_v": (6, 7), "ret_t": (6, 7), "mean": ()}
    blocks_of = {"turn": 0, "att_s": 0, "att_t": 0, "att_o": 0, "mean": 0, "mix": 0, "ret_s": 0,
                 "ret_v": 0, "ret_t": 0, "v": 2}
    used = [0] * 8
    block, projected, steps = 0, 0, []
    for kind, i in order:
        if kind == "turn":
            banks = (6, 7) if i % 2 == 0 else (2, 3)
        elif kind == "mix":
            banks = (3 - i % 2,)
        elif kind == "att_o" and i == 2:
            banks = (1,)
        elif kind in ("att_s", "att_t") and i == HEADS - 1:
            banks = (4, 5)
        elif kind in fixed:
            banks = fixed[kind]
        else:
            banks = (projected % 2,)
            projected += 1
        first = kind != "mem_v" or i == 0
        steps.append((kind, i, block, tuple((b, used[b] - (0 if first else 1)) for b in banks)))
        if first:
            for b in banks:
                used[b] += 1
        block += blocks_of.get(kind, 1)
    return steps, block, used


LAST_TURN = ("ret_t", HEADS - 1)
BLOCK_STEPS = ("mem_k", "mem_v", "mem_q", "pool", "q", "k", "v", "g")
LATE = 16 * 8


class Tally:

    def __init__(self):
        self.n = 0

    def next(self):
        self.n += 1
        return self.n


def slot_of(n, merge_first, merge_blocks):
    if merge_first <= n < merge_first + merge_blocks:
        return (n - merge_first) % 5
    return n % 4


def encoder_kernel(nc, x, mem, w_in, ret_decay_logit, w_ret_o, w_pool_grp, pool_scale, w_pool_o,
                   w_mem_kv, w_mem_o, w_out, w_ff1, w_ff2, norm1_g, norm2_g, mem_norm_g,
                   final_norm_g, identity, cos_table, sin_table, distance, inv_count, out):
    STEPS, MERGE0, USED_A = projection_steps()
    MERGE_BLOCKS = 5 * KD
    OUT0 = MERGE0 + MERGE_BLOCKS
    FFN0 = OUT0 + KD
    HALF = HIDDEN // P // 2
    GROUP = HALF // 2
    FFN_HALF_BLOCKS = HALF + 2 * GROUP
    BLOCKS = FFN0 + 2 * FFN_HALF_BLOCKS
    slots = [slot_of(n, MERGE0, MERGE_BLOCKS) for n in range(BLOCKS)]
    loads = [slots[:n + 1].count(slots[n]) for n in range(BLOCKS)]
    FF1_BANKS = ((0, 1), (2, 3))
    FF2_BANKS = (((2, 3, 4, 5), (6, 7, 0, 1)), ((4, 5, 6, 7), (0, 1, 2, 3)))

    OUT_GROUPS, OUT_COLS = 4, D // 4
    OUT_BANKS, X1_BANKS = ((6, 7, 0, 1), (4, 5), (0, 1), (4, 5, 6, 7)), (2, 3)

    used_merge = list(USED_A)
    used_out = [u + (KD if b < 6 else 0) for b, u in enumerate(used_merge)]
    out_uses, used_ffn = [], list(used_out)
    for q in range(OUT_GROUPS):
        out_uses.append({b: used_ffn[b] for b in OUT_BANKS[q]})
        for b in OUT_BANKS[q]:
            used_ffn[b] += TT // len(OUT_BANKS[q])
    for b in X1_BANKS:
        used_ffn[b] += OUT_GROUPS

    ff1_uses, ffn_uses, at_now = [], [], list(used_ffn)
    for half in range(2):
        ff1_uses.append([at_now[b] for b in FF1_BANKS[half]])
        for b in FF1_BANKS[half]:
            at_now[b] += HALF // 2
        ffn_uses.append([])
        for f in range(2):
            ffn_uses[half].append([at_now[b] for b in FF2_BANKS[half][f]])
            for b in FF2_BANKS[half][f]:
                at_now[b] += 1
    ctx = ExitStack()
    with ctx:
        BASE = 16512

        def at(name, kb, shape, dtype=FP32):
            size = int(np.prod(shape[1:])) * 4
            assert BASE + kb * KB + size <= 229344, name
            return nc.alloc_sbuf_tensor_at(name, shape, dtype, offset=int(BASE + kb * KB))

        def sem(name):
            return ctx.enter_context(nc.semaphore(name))

        h_hi, h_lo = at("h_hi", 0, [P, KD, S], FP32R), at("h_lo", 16, [P, KD, S], FP32R)
        w_hi = [at(f"w_hi{s}", 32 + 4 * s, [P, BLOCK], FP32R) for s in range(RING)]
        w_lo = [at(f"w_lo{s}", 52 + 4 * s, [P, BLOCK], FP32R) for s in range(RING)]
        w_raw = [at(f"w_raw{s}", 72 + 4 * s, [P, BLOCK]) for s in range(RING)]
        swapped, work_a = at("swapped", 48, [P, S]), at("work_a", 50, [P, S])
        work_b, sig_g = at("work_b", 68, [P, S]), at("sig_g", 70, [P, S])
        square_junk, o_nat = at("square_junk", 88, [P, D]), at("o_nat", 88, [P, TT, VD])
        memT_hi, memT_lo = at("memT_hi", 92, [P, KD, M], FP32R), at("memT_lo", 108, [P, KD, M], FP32R)
        memK_hi, memK_lo = at("memK_hi", 100, [P, HEADS, M], FP32R), at("memK_lo", 116, [P, HEADS, M], FP32R)
        memV_hi, memV_lo = at("memV_hi", 104, [P, MT, S], FP32R), at("memV_lo", 120, [P, MT, S], FP32R)
        probT_hi, probT_lo = at("probT_hi", 92, [P, MT, S], FP32R), at("probT_lo", 108, [P, MT, S], FP32R)
        probs = at("probs", 96, [P, TT, M])
        ret_hi, ret_lo = at("ret_hi", 92, [P, KD, S], FP32R), at("ret_lo", 108, [P, KD, S], FP32R)
        mq_hi, mq_lo = at("mq_hi", 124, [P, HEADS, S], FP32R), at("mq_lo", 132, [P, HEADS, S], FP32R)
        att_hi, att_lo = at("att_hi", 124, [P, HEADS, S], FP32R), at("att_lo", 132, [P, HEADS, S], FP32R)
        pool_hi, pool_lo = at("pool_hi", 140, [P, 4, S], FP32R), at("pool_lo", 148, [P, 4, S], FP32R)
        stage = [at(f"stage{s}", 156 + 4 * s, [P, D]) for s in range(MT + TT)]
        grp_raw = at("grp_raw", 68, [P, 4, P])
        grp_hi, grp_lo = at("grp_hi", 70, [P, 4, P], FP32R), at("grp_lo", 205, [P, 4, P], FP32R)
        mix_hi = [at(f"mix_hi{s}", 164 + 2 * s, [P, S], FP32R) for s in range(2)]
        mix_lo = [at(f"mix_lo{s}", 168 + 2 * s, [P, S], FP32R) for s in range(2)]
        padded = [at("padded_even", 156, [P, S + 2 * PAD]), at("padded_odd", 172, [P, S + 2 * PAD])]
        sums = [at(f"sums{s}", 174.125 + 2.125 * s, [P, S + 2 * PAD]) for s in range(2)]
        counts = at("counts", 180, [P, 4, S])
        qk_hi, qk_lo = at("qk_hi", 156, [P, 2, S], FP32R), at("qk_lo", 160, [P, 2, S], FP32R)
        v_hi, v_lo = at("v_hi", 164, [P, TT, VD], FP32R), at("v_lo", 168, [P, TT, VD], FP32R)
        s_hi, s_lo = at("s_hi", 172, [P, TT, S], FP32R), at("s_lo", 180, [P, TT, S], FP32R)
        decay_a, decay_b = at("decay_a", 172, [P, SPAN]), at("decay_b", 176, [P, SPAN])
        mrg_hi, mrg_lo = at("mrg_hi", 156, [P, KD, S], FP32R), at("mrg_lo", 172, [P, KD, S], FP32R)
        ident = at("ident", 188, [P, P])
        cos, sin = at("cos", 189, [P, S]), at("sin", 191, [P, S])
        dist, decay = at("dist", 193, [P, SPAN]), at("decay", 197, [P, SPAN])
        gate_g, work_c = at("gate_g", 201, [P, 2, S]), at("work_c", 205, [P, S])
        gain_x, gain_mem = at("gain_x", 197, [P, D]), at("gain_mem", 201, [P, D])
        gain_rows, ones_row = at("gain_rows", 16, [1, 2, D]), at("ones_row", 24, [1, P])
        sig = [at("sig_ret", 189, [P, S]), at("sig_pool", 191, [P, S]), at("sig_mem", 193, [P, S])]
        h2_hi, h2_lo = at("h2_hi", 92, [P, KD, S], FP32R), at("h2_lo", 108, [P, KD, S], FP32R)
        x1 = at("x1", 140, [P, TT, D])
        hid_hi, hid_lo = at("hid_hi", 0, [P, HALF, S], FP32R), at("hid_lo", 156, [P, HALF, S], FP32R)
        relu = [at("relu0", 189, [P, S]), at("relu1", 191, [P, S])]
        x1_squares = at("x1_squares", 189, [P, D])
        relu2 = [at("relu2_0", 193, [P, S]), at("relu2_1", 195, [P, S])]
        gain_f = at("gain_f", 197, [P, D])
        y = [at(f"y{t}", 92 + 4 * t, [P, D]) for t in range(TT)]
        x2g = at("x2g", 108, [P, TT, S])

        taken = [0]

        def tiny(name, n):
            taken[0] += n
            assert taken[0] <= 192
            return at(name, 207 + (taken[0] - n) * 4 / KB, [P, n])

        ssq, msq, rms = tiny("ssq", 8), tiny("msq", 8), tiny("rms", 8)
        minus_half = tiny("minus_half", 8)
        logit, lg_work, exp_abs = tiny("logit", 8), tiny("lg_work", 8), tiny("exp_abs", 8)
        lg_z, lg_z2, log_g = tiny("lg_z", 8), tiny("lg_z2", 8), tiny("log_g", 8)
        pscale, gain2 = tiny("pscale", 8), tiny("gain2", 8)
        row_max, row_sum, row_inv = tiny("row_max", 8), tiny("row_sum", 8), tiny("row_inv", 8)
        ret_var, ret_rstd = tiny("ret_var", 8), tiny("ret_rstd", 8)
        stats, moments = tiny("stats", 24), tiny("moments", 8)
        inv_ms, half_mean = tiny("inv_ms", 8), tiny("half_mean", 8)

        bank = [ctx.enter_context(nc.psum_tensor(f"bank{b}", [P, S], FP32)) for b in range(8)]

        stage_in = [sem(f"stage_in{s}") for s in range(MT + TT)]
        ident_in, late_in, gain_in = sem("ident_in"), sem("late_in"), sem("gain_in")
        gain_row_in = [sem("gain_row_in_mem"), sem("gain_row_in_x")]
        gains_spread, gains_copied = sem("gains_spread"), sem("gains_copied")
        grp_rounded, grp_split, mix_done = sem("grp_rounded"), sem("grp_split"), sem("mix_done")
        raw_in = [sem(f"raw_in{s}") for s in range(RING)]
        x_in = sem("x_in")
        stored, slots_cleared = sem("stored"), sem("slots_cleared")
        hi_split, lo_split = sem("hi_split"), sem("lo_split")
        blocks_done = sem("blocks_done")
        bank_free = [sem(f"bank_free{b}") for b in range(8)]
        hi_written = sem("hi_written")
        to_round = sem("to_round")
        consts_set = sem("consts_set")
        squares_summed, msq_set, rms_set = sem("squares_summed"), sem("msq_set"), sem("rms_set")
        normed = sem("normed")
        turned = sem("turned")
        scores_done, probs_turned, att_done = sem("scores_done"), sem("probs_turned"), sem("att_done")
        max_set, probs_set = sem("max_set"), sem("probs_set")
        logit_abs, logit_exp = sem("logit_abs"), sem("logit_exp")
        mixed, pads_set = sem("mixed"), sem("pads_set")
        sums_done = sem("sums_done")
        halves_swapped, sin_done = sem("halves_swapped"), sem("sin_done")
        qk_ready = sem("qk_ready")
        log_decay_set, decay_set = sem("log_decay_set"), sem("decay_set")
        ret_scores_done, s_ready, ret_values_done = sem("ret_scores_done"), sem("s_ready"), sem("ret_values_done")
        var_set, rstd_set = sem("var_set"), sem("rstd_set")
        ret_turned, ret_ready = sem("ret_turned"), sem("ret_ready")
        sigmoid_g = sem("sigmoid_g")
        merged_ready = sem("merged_ready")
        out_done, x1_turned, hid_ready = sem("out_done"), sem("x1_turned"), sem("hid_ready")
        half_sums, tokens_done = sem("half_sums"), sem("tokens_done")
        y_ready = [sem("y_ready0"), sem("y_ready1")]
        vec_step, pool_step = sem("vec_step"), sem("pool_step")

        banks_of = {(kind, i): banks for kind, i, _, banks in STEPS}

        w_in_v = w_in.rearrange("l (k p) n -> (l p) k n", p=P)
        kv_v = w_mem_kv.rearrange("l (k p) n -> (l p) k n", p=P)
        ret_o_v = w_ret_o.rearrange("l (k p) n -> (l p) k n", p=P)
        pool_o_v = w_pool_o.rearrange("l (k p) n -> (l p) k n", p=P)
        mem_o_v = w_mem_o.rearrange("l (k p) n -> (l p) k n", p=P)
        out_v = w_out.rearrange("l (k p) n -> (l p) k n", p=P)
        ff1_v = w_ff1.rearrange("l (k p) n -> (l p) k n", p=P)
        ff2_v = w_ff2.rearrange("l (k p) n -> (l p) k n", p=P)
        x_v = x.rearrange("b (t p) d -> (b p) t d", p=P)
        mem_v = mem.rearrange("b (t p) d -> (b p) t d", p=P)
        y_v = out.rearrange("b (t p) d -> (b p) t d", p=P)

        def r32(ap):
            return ap.bitcast(FP32)

        block = ctx.enter_context(nc.Block())

        @block.sync
        def _(sp):
            def load(n, view, k0, k1, col, width, turn=0):
                if n >= DEPTH:
                    sp.wait_ge(lo_split, turn + n - DEPTH + 1)
                    if not isinstance(turn, int):
                        sp.sem_inc(slots_cleared, 1)
                sp.dma_start(w_raw[slots[n]][:, :].rearrange("p (k n) -> p k n", n=width),
                             view[:, k0:k1, bass.ds(col, width)]).then_inc(raw_in[slots[n]], 16)

            def load_constants():
                for dst, src in (
                    (pscale[:, 0:4], pool_scale.rearrange("l (g c) -> c (l g)", c=P)),
                    (gain2[:, :], norm2_g.rearrange("l (k c) -> c (l k)", c=P)),
                    (logit[:, :], ret_decay_logit.rearrange("l a h -> l (a h)").broadcast_to([P, 8])),
                    (grp_raw[:, :, :], w_pool_grp.rearrange("l g c d -> (l c) g d")),
                    (cos[:, :], cos_table), (sin[:, :], sin_table), (dist[:, :], distance),
                    (counts[:, :, :].rearrange("p g s -> p (g s)"), inv_count.broadcast_to([P, 4 * S])),
                ):
                    sp.dma_start(dst, src, allow_slow_non_contiguous=True).then_inc(late_in, 16)

            sp.dma_start(gain_rows[:, 0, :], mem_norm_g.rearrange("(a n) -> a n", a=1)).then_inc(gain_row_in[0], 16)
            sp.dma_start(stage[0][:, :], mem_v[:, 0, :]).then_inc(stage_in[0], 16)
            sp.dma_start(ident[:, :], identity).then_inc(ident_in, 16)
            sp.dma_start(gain_rows[:, 1, :], norm1_g).then_inc(gain_row_in[1], 16)
            sp.dma_start(stage[1][:, :], mem_v[:, 1, :]).then_inc(stage_in[1], 16)

            for kind, i, n, _ in STEPS:
                if kind == "mem_k":
                    load(n, kv_v, 0, KD, i * P, P)
                    if i == 3:
                        load_constants()
                elif kind == "mem_v":
                    load(n, kv_v, 2 * i, 2 * i + 2, HEADS * P, S)
                elif kind == "v":
                    load(n, w_in_v, 0, 4, COL_V + i * VD, VD)
                    load(n + 1, w_in_v, 4, KD, COL_V + i * VD, VD)
                elif kind in ("mem_q", "pool", "q", "k", "g"):
                    col = {"mem_q": COL_MQ, "pool": COL_POOL, "q": COL_Q, "k": COL_K, "g": COL_G}[kind]
                    load(n, w_in_v, 0, KD, col + i * P, P)
                if kind in ("mem_k", "mem_v") and 2 <= n < 2 + TT:
                    t = n - 2
                    sp.dma_start(stage[MT + t][:, :], x_v[:, t, :]).then_inc(stage_in[MT + t], 16)

            def load_gates(m, shift, turn):
                for b in range(N_BRANCHES):
                    load(MERGE0 + 5 * shift + b, w_in_v, 0, KD, COL_GATES + b * D + m * P, P, turn)
                load(MERGE0 + 5 * shift + 3, ret_o_v, 0, KD, m * P, P, turn)

            def load_pool_mem(m, turn):
                n = MERGE0 + 4
                sp.wait_ge(lo_split, turn + n - DEPTH + 1)
                if not isinstance(turn, int):
                    sp.sem_inc(slots_cleared, 1)
                raw = w_raw[slots[n]]
                sp.dma_start(raw[:, 0:S].rearrange("p (k n) -> p k n", n=P),
                             pool_o_v[:, :, bass.ds(m * P, P)]).then_inc(raw_in[slots[n]], 16)
                sp.dma_start(raw[:, S:BLOCK].rearrange("p (k n) -> p k n", n=P),
                             mem_o_v[:, :, bass.ds(m * P, P)]).then_inc(raw_in[slots[n]], 16)

            load_gates(0, 0, 0)
            sp.wait_ge(ret_ready, KD)
            with sp.Fori(0, KD - 1) as m:
                load_pool_mem(m, 5 * m)
                load_gates(m + 1, 1, 5 * m)
            load_pool_mem(KD - 1, 5 * (KD - 1))

            for m in range(KD):
                q, b = m // 2, m % 2
                load(OUT0 + m, out_v, 4 * b, 4 * b + 4, q * OUT_COLS, OUT_COLS)
                if m == 4:
                    sp.wait_ge(blocks_done, OUT0)
                    for t in range(TT):
                        sp.dma_start(x1[:, t, :], x_v[:, t, :]).then_inc(x_in, 16)

            for half in range(2):
                n0 = FFN0 + half * FFN_HALF_BLOCKS
                with sp.Fori(0, HALF // 4) as q:
                    for jj in range(4):
                        load(n0 + jj, ff1_v, 0, KD, q * (4 * P) + (half * HALF + jj) * P, P, 4 * q)
                if half == 0:
                    sp.dma_start(gain_f[:, :], final_norm_g.rearrange("(a n) -> a n", a=1).broadcast_to([P, D]))\
                        .then_inc(gain_in, 16)
                for f in range(2):
                    for b in range(GROUP):
                        k = half * HALF + 2 * b
                        load(n0 + HALF + f * GROUP + b, ff2_v, k, k + 2, f * S, S)

            for t in range(TT):
                sp.wait_ge(y_ready[0], t + 1)
                sp.wait_ge(y_ready[1], t + 1)
                sp.dma_start(y_v[:, t, :], y[t][:, :]).then_inc(stored, 16)
            sp.wait_ge(stored, 16 * TT)

        @block.tensor
        def _(pe):
            def three(out_ap, wh, wl, xh, xl, first, last):
                pe.matmul(out_ap, wh, xh, start=first, stop=False)
                pe.matmul(out_ap, wh, xl, start=False, stop=False)
                return pe.matmul(out_ap, wl, xh, start=False, stop=last)

            def project(s, out_ap, x_hi, x_lo, tiles, w0=0, tile_ready=None):
                for k in range(tiles):
                    if tile_ready is not None:
                        pe.wait_ge(*tile_ready(k))
                    c = slice((w0 + k) * P, (w0 + k + 1) * P)
                    last = three(out_ap, w_hi[s][:, c], w_lo[s][:, c], x_hi[:, k, :], x_lo[:, k, :],
                                 k == 0, k == tiles - 1)
                return last

            def free(b, uses):
                if uses:
                    pe.wait_ge(bank_free[b], uses)

            def read_out(kind, i):
                for b, uses in banks_of[kind, i]:
                    pe.wait_ge(bank_free[b], uses + 1)

            def turn_back_head(i, banks):
                read_out("ret_v", i)
                for c in range(2):
                    for t in range(TT):
                        last = pe.transpose(bank[banks[c][0]][:, t * P:(t + 1) * P],
                                            o_nat[:, t, c * P:(c + 1) * P], ident[:, :])
                    last.then_inc(ret_turned, 1)

            def spread_gain(g, c):
                pe.wait_ge(gain_row_in[g], 16)
                if g:
                    pe.wait_ge(gains_copied, c + 1)
                pe.matmul(bank[c][:, :], ones_row[:, :], gain_rows[:, g, c * S:(c + 1) * S],
                          start=True, stop=True).then_inc(gains_spread, 1)

            pe.wait_ge(consts_set, 2)
            spread_gain(0, 0)
            spread_gain(0, 1)
            spread_gain(1, 0)
            pe.wait_ge(ident_in, 16)
            for kind, i, n, banks in STEPS:
                if (kind, i) == LAST_TURN:
                    continue
                for b, uses in banks:
                    if kind != "mem_v" or i == 0:
                        free(b, uses)
                if kind == "turn":
                    pe.wait_ge(normed, i + 1)
                    for c, (b, _) in enumerate(banks):
                        for k in range(4):
                            f = (4 * c + k) * P
                            last = pe.transpose(bank[b][:, k * P:(k + 1) * P], stage[i][:, f:f + P], ident[:, :])
                        last.then_inc(turned, 1)
                elif kind == "mem_k":
                    pe.wait_ge(lo_split, n + 1)
                    if i == 0:
                        pe.wait_ge(gains_copied, 4)
                    project(slots[n], bank[banks[0][0]][:, 0:M], memT_hi, memT_lo, KD).then_inc(blocks_done, 1)
                elif kind == "mem_v":
                    pe.wait_ge(lo_split, n + 1)
                    for t in range(MT):
                        if i == 0:
                            if t == 1:
                                spread_gain(1, 1)
                            read_out("turn", t)
                        for kk in range(2):
                            k = 2 * i + kk
                            c = slice(kk * S, (kk + 1) * S)
                            tok = slice(t * P, (t + 1) * P)
                            last = three(bank[banks[t][0]][:, :], memT_hi[:, k, tok], memT_lo[:, k, tok],
                                         w_hi[slots[n]][:, c], w_lo[slots[n]][:, c], k == 0, k == KD - 1)
                    last.then_inc(blocks_done, 1)
                elif kind in ("mem_q", "pool", "q", "k", "g"):
                    pe.wait_ge(lo_split, n + 1)
                    if kind == "mem_q" and i == 0:
                        for t in range(MT, MT + TT):
                            read_out("turn", t)
                    project(slots[n], bank[banks[0][0]][:, :], h_hi, h_lo, KD).then_inc(blocks_done, 1)
                elif kind == "v":
                    pe.wait_ge(lo_split, n + 1)
                    for t in range(TT):
                        tok = slice(t * P, (t + 1) * P)
                        dst = bank[banks[t // 2][0]][:, (t % 2) * VD:(t % 2 + 1) * VD]
                        for k in range(KD):
                            s, c = slots[n + k // 4], slice((k % 4) * VD, (k % 4 + 1) * VD)
                            if t == 0 and k == 4:
                                pe.wait_ge(lo_split, n + 2)
                            last = three(dst, h_hi[:, k, tok], h_lo[:, k, tok], w_hi[s][:, c], w_lo[s][:, c],
                                         k == 0, k == KD - 1)
                            if t == TT - 1 and k == KD - 2:
                                last.then_inc(blocks_done, 1)
                    last.then_inc(blocks_done, 1)
                elif kind == "mix":
                    pe.wait_ge(mixed, i + 1)
                    pe.wait_ge(grp_split, 1)
                    b = banks[0][0]
                    three(bank[b][:, :], grp_hi[:, i, :], grp_lo[:, i, :], mix_hi[i % 2][:, :],
                          mix_lo[i % 2][:, :], True, True).then_inc(mix_done, 1)
                elif kind == "att_s":
                    read_out("mem_q", i)
                    for t in range(TT):
                        tok = slice(t * P, (t + 1) * P)
                        last = three(bank[banks[t // 2][0]][:, (t % 2) * M:(t % 2 + 1) * M],
                                     mq_hi[:, i, tok], mq_lo[:, i, tok], memK_hi[:, i, :], memK_lo[:, i, :],
                                     True, True)
                    last.then_inc(scores_done, 1)
                elif kind == "att_t":
                    pe.wait_ge(probs_set, i + 1)
                    for c in range(MT):
                        for t in range(TT):
                            last = pe.transpose(bank[banks[c][0]][:, t * P:(t + 1) * P],
                                                probs[:, t, c * P:(c + 1) * P], ident[:, :])
                    last.then_inc(probs_turned, 1)
                elif kind == "att_o":
                    if i == 0:
                        read_out("mem_v", 0)
                    read_out("att_t", i)
                    for c in range(MT):
                        d = slice(i * P, (i + 1) * P)
                        last = three(bank[banks[0][0]][:, :], memV_hi[:, c, d], memV_lo[:, c, d],
                                     probT_hi[:, c, :], probT_lo[:, c, :], c == 0, c == MT - 1)
                    last.then_inc(att_done, 1)
                elif kind == "ret_s":
                    hd, p = i // 2, i % 2
                    pe.wait_ge(qk_ready, 2 * hd + 2)
                    for jj in range(2):
                        j = 2 * p + jj
                        last = three(bank[banks[jj][0]][:, :], qk_hi[:, 1, j * P:(j + 1) * P],
                                     qk_lo[:, 1, j * P:(j + 1) * P], qk_hi[:, 0, :], qk_lo[:, 0, :], True, True)
                        last.then_inc(ret_scores_done, 1)
                elif kind == "ret_v":
                    pe.wait_ge(s_ready, 4 * i + 4)
                    read_out("v", i)
                    for t in range(TT):
                        tok = slice(t * P, (t + 1) * P)
                        for j in range(TT):
                            last = three(bank[banks[t // 2][0]][:, (t % 2) * VD:(t % 2 + 1) * VD],
                                         s_hi[:, j, tok], s_lo[:, j, tok], v_hi[:, j, :], v_lo[:, j, :],
                                         j == 0, j == TT - 1)
                    last.then_inc(ret_values_done, 1)
                elif kind == "ret_t":
                    turn_back_head(i, banks)

            for i in range(4):
                read_out("mix", i)
                read_out("att_o", i)
            def merge_tile(m, first=False):
                for g in range(N_BRANCHES):
                    pe.wait_ge(lo_split, 5 * m + MERGE0 + g + 1)
                    pe.wait_ge(bank_free[g], m + used_merge[g])
                    project(g, bank[g][:, :], h_hi, h_lo, KD).then_inc(blocks_done, 1)
                    if first and g == 0:
                        for b, uses in banks_of[LAST_TURN]:
                            free(b, uses)
                        turn_back_head(HEADS - 1, banks_of[LAST_TURN])
                pe.wait_ge(lo_split, 5 * m + MERGE0 + 4)
                pe.wait_ge(bank_free[3], m + used_merge[3])
                pe.wait_ge(ret_ready, KD)
                project(3, bank[3][:, :], ret_hi, ret_lo, KD).then_inc(blocks_done, 1)
                pe.wait_ge(lo_split, 5 * m + MERGE0 + 5)
                pe.wait_ge(bank_free[4], m + used_merge[4])
                project(4, bank[4][:, :], pool_hi, pool_lo, 4)
                pe.wait_ge(bank_free[5], m + used_merge[5])
                project(4, bank[5][:, :], att_hi, att_lo, 4, 4).then_inc(blocks_done, 1)

            merge_tile(0, first=True)
            with pe.Fori(1, KD) as m:
                merge_tile(m)

            def out_part(q, t, b):
                s, tok = slots[OUT0 + 2 * q + b], slice(t * P, (t + 1) * P)
                four = len(OUT_BANKS[q]) == TT
                dst, c0 = bank[OUT_BANKS[q][t if four else t // 2]], 0 if four else (t % 2) * OUT_COLS
                for kk in range(4):
                    k, c = 4 * b + kk, slice(kk * OUT_COLS, (kk + 1) * OUT_COLS)
                    if q == t == 0:
                        pe.wait_ge(merged_ready, k + 2)
                    last = three(dst[:, c0:c0 + OUT_COLS], mrg_hi[:, k, tok], mrg_lo[:, k, tok],
                                 w_hi[s][:, c], w_lo[s][:, c], k == 0, k == KD - 1)
                if t == TT - 1:
                    last.then_inc(blocks_done, 1)
                elif b == 1:
                    last.then_inc(out_done, 1)

            def turn_x1(q):
                for b in X1_BANKS:
                    free(b, used_out[b] + q)
                for t in range(TT):
                    four = len(OUT_BANKS[q]) == TT
                    b = OUT_BANKS[q][t if four else t // 2]
                    pe.wait_ge(bank_free[b], out_uses[q][b] + (1 if four else t % 2 + 1))
                    for c in range(2):
                        f = q * OUT_COLS + c * P
                        last = pe.transpose(bank[X1_BANKS[c]][:, t * P:(t + 1) * P], x1[:, t, f:f + P], ident[:, :])
                        if t == TT - 1:
                            last.then_inc(x1_turned, 1)

            for q in range(OUT_GROUPS):
                for b in OUT_BANKS[q]:
                    free(b, out_uses[q][b])
                for b in range(2) if q == 0 else ():
                    pe.wait_ge(lo_split, OUT0 + b + 1)
                    for t in range(TT):
                        out_part(q, t, b)
                for t in range(TT) if q else ():
                    for b in range(2):
                        if t == 0:
                            pe.wait_ge(lo_split, OUT0 + 2 * q + b + 1)
                        out_part(q, t, b)
                    if t == 0:
                        turn_x1(q - 1)
            turn_x1(OUT_GROUPS - 1)

            def h2_tile(k):
                return bank_free[X1_BANKS[k % 2]], used_out[X1_BANKS[k % 2]] + k // 2 + 1

            uses = list(used_ffn)
            for half in range(2):
                n0 = FFN0 + half * FFN_HALF_BLOCKS
                pair = FF1_BANKS[half]
                with pe.Fori(0, HALF // 4) as q:
                    for jj in range(4):
                        b = pair[jj % 2]
                        pe.wait_ge(lo_split, 4 * q + n0 + jj + 1)
                        pe.wait_ge(bank_free[b], 2 * q + uses[b] + jj // 2)
                        project(slots[n0 + jj], bank[b][:, :], h2_hi, h2_lo, KD,
                                tile_ready=h2_tile if half == jj == 0 else None).then_inc(blocks_done, 1)
                for b in pair:
                    uses[b] += HALF // 2
                for f in range(2):
                    four = FF2_BANKS[half][f]
                    for b in four:
                        free(b, uses[b])
                        uses[b] += 1
                    def add_block(g, t):
                        s, tok = slots[n0 + HALF + f * GROUP + g], slice(t * P, (t + 1) * P)
                        for kk in range(2):
                            k, c = 2 * g + kk, slice(kk * S, (kk + 1) * S)
                            last = three(bank[four[t]][:, :], hid_hi[:, k, tok], hid_lo[:, k, tok],
                                         w_hi[s][:, c], w_lo[s][:, c], k == 0, k == HALF - 1)
                        return last

                    by_tokens = 2 if half == f == 1 else 0
                    for g in range(GROUP - by_tokens):
                        pe.wait_ge(lo_split, n0 + HALF + f * GROUP + g + 1)
                        pe.wait_ge(hid_ready, half * HALF + 2 * g + 2)
                        for t in range(TT):
                            last = add_block(g, t)
                        last.then_inc(blocks_done, 1)
                    if by_tokens:
                        pe.wait_ge(lo_split, BLOCKS)
                        for t in range(TT):
                            for g in range(GROUP - by_tokens, GROUP):
                                last = add_block(g, t)
                            last.then_inc(tokens_done, 1)

        @block.scalar
        def _(act):
            act.preload_act_table(ACT.Exp)

            rounds = Tally()

            def split(n, per=0, i=0):
                s = slots[n]
                act.wait_ge(raw_in[s], 32 * i + 32 if s == RING - 1 else 16 * i + 16 * loads[n])
                if n >= DEPTH:
                    act.wait_ge(blocks_done, per * i + n - DEPTH + 1)
                act.activation(w_hi[s][:, :], w_raw[s][:, :], ACT.Copy).then_inc(hi_split, 1)

            def round_to(dst, src, scale=1.0):
                act.activation(dst, src, ACT.Copy, scale=scale).then_inc(hi_written, 1)

            def square_rows(s):
                act.wait_ge(stage_in[s], 16)
                if s:
                    act.wait_ge(squares_summed, s)
                act.activation(square_junk[:, :], stage[s][:, :], ACT.Square,
                               accum_out=ssq[:, s:s + 1]).then_inc(squares_summed, 1)

            def turn_back_head(i, banks):
                for c, (b, uses) in enumerate(banks):
                    act.wait_ge(bank_free[b], uses + 1)
                    round_to(ret_hi[:, 2 * i + c, :], (work_a, work_c)[c][:, :])

            def copy_gain(g, c):
                act.wait_ge(gains_spread, 2 * g + c + 1)
                act.activation((gain_mem, gain_x)[g][:, c * S:(c + 1) * S], bank[c][:, :], ACT.Copy)\
                    .then_inc(gains_copied, 1)

            square_rows(0)
            copy_gain(0, 0)
            copy_gain(0, 1)
            square_rows(1)
            split(0)
            for kind, i, n, banks in STEPS:
                if (kind, i) == LAST_TURN:
                    continue
                b = banks[0][0] if banks else None
                if kind == "mem_v":
                    square_rows(MT + i)
                if kind in BLOCK_STEPS:
                    split(n + AHEAD)
                if kind == "turn":
                    hi = memT_hi if i < MT else h_hi
                    tok = slice((i % MT) * P, (i % MT + 1) * P) if i < MT else slice((i - MT) * P, (i - MT + 1) * P)
                    for c, (b, _) in enumerate(banks):
                        act.wait_ge(turned, 2 * i + c + 1)
                        round_to(hi[:, 4 * c:4 * c + 4, tok], bank[b][:, :].rearrange("p (k n) -> p k n", n=P))
                    if i == MT - 1:
                        split(1)
                        copy_gain(1, 0)
                        copy_gain(1, 1)
                        split(2)
                elif kind == "mem_k":
                    act.wait_ge(blocks_done, n + 1)
                    round_to(memK_hi[:, i, :], bank[b][:, 0:M])
                elif kind == "mem_v" and i == 3:
                    act.wait_ge(blocks_done, n + 1)
                    for t in range(MT):
                        round_to(memV_hi[:, t, :], bank[banks[t][0]][:, :])
                elif kind == "mem_q":
                    if i == 0:
                        act.wait_ge(logit_abs, 1)
                        act.activation(exp_abs[:, :], lg_work[:, :], ACT.Exp).then_inc(logit_exp, 1)
                        act.activation(grp_hi[:, :, :], grp_raw[:, :, :], ACT.Copy).then_inc(grp_rounded, 1)
                    act.wait_ge(blocks_done, n + 1)
                    round_to(mq_hi[:, i, :], bank[b][:, :])
                elif kind == "pool":
                    act.wait_ge(pads_set, 2)
                    act.wait_ge(blocks_done, n + 1)
                    if i >= 2:
                        act.wait_ge(mixed, i - 1)
                    act.activation(padded[i % 2][:, PAD:PAD + S], bank[b][:, :], ACT.Copy)\
                        .then_inc(bank_free[b], 1)
                elif kind == "mean":
                    act.wait_ge(to_round, rounds.next())
                    if i >= 2:
                        act.wait_ge(mix_done, i - 1)
                    round_to(mix_hi[i % 2][:, :], work_a[:, :])
                elif kind == "mix":
                    act.wait_ge(mix_done, i + 1)
                    round_to(pool_hi[:, i, :], bank[b][:, :], pscale[:, i:i + 1])
                elif kind == "att_s":
                    act.wait_ge(max_set, i + 1)
                    for t in range(TT):
                        e = act.activation(probs[:, t, :], bank[banks[t // 2][0]][:, (t % 2) * M:(t % 2 + 1) * M],
                                           ACT.Exp, bias=row_max[:, t:t + 1], scale=QK_SCALE,
                                           accum_out=row_sum[:, t:t + 1])
                        if t % 2:
                            e.then_inc(bank_free[banks[t // 2][0]], 1)
                elif kind == "att_t":
                    act.wait_ge(probs_turned, i + 1)
                    for c in range(MT):
                        round_to(probT_hi[:, c, :], bank[banks[c][0]][:, :])
                elif kind == "att_o":
                    act.wait_ge(att_done, i + 1)
                    round_to(att_hi[:, i, :], bank[b][:, :])
                elif kind in ("q", "k"):
                    act.wait_ge(blocks_done, n + 1)
                    turn = 2 * i + (kind == "k")
                    if turn:
                        act.wait_ge(sin_done, turn)
                    half = P // 2
                    act.activation(swapped[0:half, :], bank[b][half:P, :], ACT.Copy)
                    act.activation(swapped[half:P, :], bank[b][0:half, :], ACT.Copy).then_inc(halves_swapped, 1)
                    act.wait_ge(to_round, rounds.next())
                    round_to(qk_hi[:, int(kind == "k"), :], work_a[:, :])
                elif kind == "v":
                    act.wait_ge(log_decay_set, i + 1)
                    act.activation(decay[:, :], decay_a[:, :], ACT.Exp).then_inc(decay_set, 1)
                    act.wait_ge(blocks_done, n + 2)
                    for c, (b, _) in enumerate(banks):
                        round_to(v_hi[:, 2 * c:2 * c + 2, :], bank[b][:, :].rearrange("p (t e) -> p t e", e=VD))
                    split(n + 1 + AHEAD)
                elif kind == "g":
                    act.wait_ge(blocks_done, n + 1)
                    if i:
                        b0, uses = banks_of["g", i - 1][0]
                        act.wait_ge(bank_free[b0], uses + 1)
                    act.activation(sig_g[:, :], bank[b][:, :], ACT.Sigmoid).then_inc(sigmoid_g, 1)
                elif kind == "ret_s":
                    for jj, (b, uses) in enumerate(banks):
                        act.wait_ge(bank_free[b], uses + 1)
                        round_to(s_hi[:, 2 * (i % 2) + jj, :], (work_a, work_c)[jj][:, :])
                elif kind == "ret_t":
                    turn_back_head(i, banks)

            act.preload_act_table(ACT.Sigmoid)
            def merge_tile(m, first=False):
                for g in range(N_BRANCHES):
                    split(MERGE0 + AHEAD + g, 5, m)
                    act.wait_ge(blocks_done, 5 * m + MERGE0 + g + 1)
                    if g == 0:
                        act.wait_ge(merged_ready, m + 1)
                    act.activation(sig[g][:, :], bank[g][:, :], ACT.Sigmoid).then_inc(bank_free[g], 1)
                    if first and g == 0:
                        turn_back_head(HEADS - 1, banks_of[LAST_TURN])
                split(MERGE0 + AHEAD + 3, 5, m)
                split(MERGE0 + AHEAD + 4, 5, m)
                act.wait_ge(to_round, m + rounds.n + 1)
                round_to(mrg_hi[:, bass.ds(m, 1), :], sig[0][:, :].rearrange("p (a s) -> p a s", a=1))

            merge_tile(0, first=True)
            with act.Fori(1, KD) as m:
                merge_tile(m)
            rounds.n += KD

            act.wait_ge(blocks_done, OUT0)

            def round_h2(q):
                for c in range(2):
                    k = 2 * q + c
                    act.wait_ge(x1_turned, k + 1)
                    round_to(h2_hi[:, k, :], bank[X1_BANKS[c]][:, :], gain2[:, k:k + 1])

            for q in range(OUT_GROUPS):
                split(OUT0 + 2 * q + AHEAD)
                if q:
                    round_h2(q - 1)
                split(OUT0 + 2 * q + 1 + AHEAD)
            round_h2(OUT_GROUPS - 1)

            for half in range(2):
                n0 = FFN0 + half * FFN_HALF_BLOCKS
                pair = FF1_BANKS[half]
                with act.Fori(0, HALF // 4) as q:
                    for jj in range(4):
                        b = pair[jj % 2]
                        split(n0 + jj + AHEAD, 4, q)
                        act.wait_ge(blocks_done, 4 * q + n0 + jj + 1)
                        act.activation(relu[jj % 2][:, :], bank[b][:, :], ACT.Relu).then_inc(bank_free[b], 1)
                        act.wait_ge(to_round, 4 * q + rounds.n + jj + 1)
                        round_to(hid_hi[:, bass.ds(4 * q + jj, 1), :],
                                 relu2[jj % 2][:, :].rearrange("p (a s) -> p a s", a=1))
                rounds.n += HALF
                for f in range(2):
                    for g in range(GROUP):
                        n = n0 + HALF + f * GROUP + g
                        if n + AHEAD < BLOCKS:
                            split(n + AHEAD)
                        if half == f == 0 and g < TT:
                            act.wait_ge(squares_summed, MT + TT + g)
                            act.activation(x1_squares[:, :], x1[:, g, :], ACT.Square,
                                           accum_out=ssq[:, g:g + 1]).then_inc(squares_summed, 1)
                    if half == f == 0:
                        act.wait_ge(squares_summed, MT + TT + TT)
                    if half == 1:
                        for t in range(TT):
                            b = FF2_BANKS[half][f][t]
                            act.wait_ge(bank_free[b], ffn_uses[half][f][t] + 1)
                            if 4 * f + t:
                                act.wait_ge(half_sums, 4 * f + t)
                            act.activation(relu[t % 2][:, :], x1[:, t, f * S:(f + 1) * S], ACT.Square,
                                           accum_out=ssq[:, 4 * f + t:4 * f + t + 1]).then_inc(half_sums, 1)
                            if f == 1:
                                act.wait_ge(rms_set, MT + TT + t + 1)
                                act.activation(y[t][:, 0:S], x2g[:, t, :], ACT.Copy, scale=rms[:, t:t + 1])\
                                    .then_inc(y_ready[0], 1)

        @block.vector
        def _(dve):
            rounded, steps = Tally(), Tally()

            def link(ins):
                ins.then_inc(vec_step, 1)
                dve.wait_ge(vec_step, steps.next())

            def past(counter, value):
                if value > 0:
                    dve.wait_ge(counter, value)

            def split(n, per=0, i=0):
                s = slots[n]
                dve.wait_ge(hi_split, per * i + n + 1)
                dve.tensor_tensor(w_lo[s][:, :], w_raw[s][:, :], r32(w_hi[s][:, :]), ALU.subtract)\
                    .then_inc(lo_split, 1)

            def rest(dst, src, hi, scale=None):
                dve.wait_ge(hi_written, rounded.next())
                if scale is None:
                    return dve.tensor_tensor(dst, src, r32(hi), ALU.subtract)
                return dve.scalar_tensor_tensor(out=dst, in0=src, scalar=scale, in1=r32(hi),
                                                op0=ALU.mult, op1=ALU.subtract)

            def mean_square(s):
                dve.wait_ge(squares_summed, s + 1)
                dve.tensor_scalar(msq[:, s:s + 1], ssq[:, s:s + 1], 1.0 / D, EPS, ALU.mult, ALU.add)\
                    .then_inc(msq_set, 1)

            def norm_rows(s, gain, copied):
                dve.wait_ge(rms_set, s + 1)
                dve.wait_ge(gains_copied, copied)
                dve.scalar_tensor_tensor(out=stage[s][:, :], in0=stage[s][:, :], scalar=rms[:, s:s + 1],
                                         in1=gain[:, :], op0=ALU.mult, op1=ALU.mult).then_inc(normed, 1)

            def log_sigmoid():
                dve.wait_ge(late_in, LATE)
                link(dve.tensor_scalar(lg_work[:, :], logit[:, :], -1.0, None, ALU.mult))
                dve.tensor_tensor(lg_work[:, :], lg_work[:, :], logit[:, :], ALU.min).then_inc(logit_abs, 1)
                dve.wait_ge(logit_exp, 1)
                link(dve.tensor_scalar(lg_z[:, :], exp_abs[:, :], 2.0, None, ALU.add))
                link(dve.reciprocal(lg_z[:, :], lg_z[:, :]))
                link(dve.tensor_tensor(lg_z[:, :], lg_z[:, :], exp_abs[:, :], ALU.mult))
                link(dve.tensor_tensor(lg_z2[:, :], lg_z[:, :], lg_z[:, :], ALU.mult))
                link(dve.tensor_scalar(log_g[:, :], lg_z2[:, :], 1.0 / 17, None, ALU.mult))
                for odd in range(15, 0, -2):
                    link(dve.scalar_tensor_tensor(out=log_g[:, :], in0=log_g[:, :], scalar=1.0 / odd,
                                                  in1=(lg_z2 if odd > 1 else lg_z)[:, :],
                                                  op0=ALU.add, op1=ALU.mult))
                link(dve.tensor_scalar(lg_work[:, :], logit[:, :], 0.0, None, ALU.min))
                link(dve.scalar_tensor_tensor(out=log_g[:, :], in0=log_g[:, :], scalar=-2.0,
                                              in1=lg_work[:, :], op0=ALU.mult, op1=ALU.add))

            def window_means(i):
                dve.wait_ge(sums_done, i + 1)
                past(mixed, i)
                link(dve.tensor_tensor(work_a[:, :], sums[i % 2][:, PAD:PAD + S], counts[:, i, :], ALU.mult))
                dve.tensor_tensor(work_a[:, :], work_a[:, :], padded[i % 2][:, PAD:PAD + S], ALU.subtract)\
                    .then_inc(to_round, 1)
                rest(mix_lo[i % 2][:, :], work_a[:, :], mix_hi[i % 2][:, :]).then_inc(mixed, 1)

            def turn_back_head(i, banks):
                b0, uses = banks_of["g", 2 * i + 1][0]
                dve.wait_ge(bank_free[b0], uses + 1)
                for c, (b, _) in enumerate(banks):
                    dve.wait_ge(ret_turned, 2 * i + c + 1)
                    past(s_ready, 4 * i + 4)
                    past(qk_ready, min(2 * i + 4, 2 * HEADS))
                    dve.tensor_tensor((work_a, work_c)[c][:, :], bank[b][:, :], gate_g[:, c, :], ALU.mult)\
                        .then_inc(bank_free[b], 1)
                for c in range(2):
                    rest(ret_lo[:, 2 * i + c, :], (work_a, work_c)[c][:, :], ret_hi[:, 2 * i + c, :])\
                        .then_inc(ret_ready, 1)

            for s in range(MT):
                mean_square(s)
                norm_rows(s, gain_mem, 2)
            for kind, i, n, banks in STEPS:
                if (kind, i) == LAST_TURN:
                    continue
                b = banks[0][0] if banks else None
                if kind == "mem_v":
                    mean_square(MT + i)
                if kind in BLOCK_STEPS:
                    split(n + AHEAD)
                if kind == "turn":
                    hi, lo = (memT_hi, memT_lo) if i < MT else (h_hi, h_lo)
                    tok = slice(i * P, (i + 1) * P) if i < MT else slice((i - MT) * P, (i - MT + 1) * P)
                    for c, (b, _) in enumerate(banks):
                        rest(lo[:, 4 * c:4 * c + 4, tok], bank[b][:, :].rearrange("p (k n) -> p k n", n=P),
                             hi[:, 4 * c:4 * c + 4, tok]).then_inc(bank_free[b], 1)
                    if i == MT - 1:
                        dve.wait_ge(lo_split, 1)
                        split(1)
                        split(2)
                elif kind == "mem_k":
                    rest(memK_lo[:, i, :], bank[b][:, 0:M], memK_hi[:, i, :]).then_inc(bank_free[b], 1)
                elif kind == "mem_v":
                    norm_rows(MT + i, gain_x, 4)
                    if i == 3:
                        for t in range(MT):
                            b = banks[t][0]
                            rest(memV_lo[:, t, :], bank[b][:, :], memV_hi[:, t, :]).then_inc(bank_free[b], 1)
                elif kind == "mem_q":
                    if i == 0:
                        log_sigmoid()
                        dve.wait_ge(grp_rounded, 1)
                        dve.tensor_tensor(grp_lo[:, :, :], grp_raw[:, :, :], r32(grp_hi[:, :, :]), ALU.subtract)\
                            .then_inc(grp_split, 1)
                    rest(mq_lo[:, i, :], bank[b][:, :], mq_hi[:, i, :]).then_inc(bank_free[b], 1)
                elif kind == "mean":
                    window_means(i)
                elif kind == "mix":
                    rest(pool_lo[:, i, :], bank[b][:, :], pool_hi[:, i, :], pscale[:, i:i + 1]).then_inc(bank_free[b], 1)
                elif kind == "att_s":
                    dve.wait_ge(scores_done, i + 1)
                    for c, (b, _) in enumerate(banks):
                        link(dve.tensor_reduce(row_max[:, 2 * c:2 * c + 2],
                                               bank[b][:, :].rearrange("p (t m) -> p t m", m=M), AX.X, ALU.max))
                    dve.tensor_scalar(row_max[:, 0:4], row_max[:, 0:4], -QK_SCALE, None, ALU.mult).then_inc(max_set, 1)
                    for b, uses in banks:
                        dve.wait_ge(bank_free[b], uses + 1)
                    link(dve.reciprocal(row_inv[:, 0:4], row_sum[:, 0:4]))
                    for t in range(TT):
                        ins = dve.tensor_scalar(probs[:, t, :], probs[:, t, :], row_inv[:, t:t + 1], None, ALU.mult)
                    ins.then_inc(probs_set, 1)
                elif kind == "att_t":
                    for c, (b, _) in enumerate(banks):
                        rest(probT_lo[:, c, :], bank[b][:, :], probT_hi[:, c, :]).then_inc(bank_free[b], 1)
                elif kind == "att_o":
                    rest(att_lo[:, i, :], bank[b][:, :], att_hi[:, i, :]).then_inc(bank_free[b], 1)
                elif kind in ("q", "k"):
                    turn = 2 * i + (kind == "k")
                    dve.wait_ge(halves_swapped, turn + 1)
                    past(mixed, 4)
                    past(qk_ready, turn)
                    past(s_ready, 4 * i)
                    past(ret_ready, 2 * i - 2)
                    dve.tensor_tensor(work_a[:, :], bank[b][:, :], cos[:, :], ALU.mult).then_inc(bank_free[b], 1)
                    dve.wait_ge(bank_free[b], banks[0][1] + 1)
                    dve.wait_ge(sin_done, turn + 1)
                    dve.tensor_tensor(work_a[:, :], work_a[:, :], work_b[:, :], ALU.add).then_inc(to_round, 1)
                    c = int(kind == "k")
                    rest(qk_lo[:, c, :], work_a[:, :], qk_hi[:, c, :]).then_inc(qk_ready, 1)
                elif kind == "v":
                    if i:
                        dve.wait_ge(ret_values_done, i)
                    dve.tensor_scalar(decay_a[:, :], dist[:, :], 0.0, log_g[:, i:i + 1], ALU.max, ALU.mult)
                    link(dve.tensor_scalar(decay_b[:, :], dist[:, :], 0.0, log_g[:, 4 + i:5 + i],
                                           ALU.min, ALU.mult))
                    dve.tensor_tensor(decay_a[:, :], decay_a[:, :], decay_b[:, :], ALU.subtract)\
                        .then_inc(log_decay_set, 1)
                    for c, (b, _) in enumerate(banks):
                        rest(v_lo[:, 2 * c:2 * c + 2, :], bank[b][:, :].rearrange("p (t e) -> p t e", e=VD),
                             v_hi[:, 2 * c:2 * c + 2, :]).then_inc(bank_free[b], 1)
                    split(n + 1 + AHEAD)
                elif kind == "g":
                    dve.wait_ge(sigmoid_g, i + 1)
                    dve.tensor_tensor(gate_g[:, i % 2, :], sig_g[:, :], bank[b][:, :], ALU.mult)\
                        .then_inc(bank_free[b], 1)
                elif kind == "ret_s":
                    dve.wait_ge(decay_set, i // 2 + 1)
                    for jj, (b, _) in enumerate(banks):
                        j = 2 * (i % 2) + jj
                        dve.wait_ge(ret_scores_done, 2 * i + jj + 1)
                        past(s_ready, 2 * i)
                        past(qk_ready, 2 * (i // 2) + 2)
                        past(ret_ready, 2 * (i // 2))
                        dve.scalar_tensor_tensor(out=(work_a, work_c)[jj][:, :], in0=bank[b][:, :],
                                                 scalar=QK_SCALE, in1=decay[:, REACH - j * P:REACH - j * P + S],
                                                 op0=ALU.mult, op1=ALU.mult).then_inc(bank_free[b], 1)
                    for jj in range(2):
                        j = 2 * (i % 2) + jj
                        rest(s_lo[:, j, :], (work_a, work_c)[jj][:, :], s_hi[:, j, :]).then_inc(s_ready, 1)
                elif kind == "ret_v":
                    dve.wait_ge(ret_values_done, i + 1)
                    for t in range(TT):
                        ins = dve.bn_stats(stats[:, 6 * t:6 * t + 6],
                                           bank[banks[t // 2][0]][:, (t % 2) * VD:(t % 2 + 1) * VD])
                    link(ins)
                    for t in range(TT):
                        ins = dve.bn_aggr(moments[:, 2 * t:2 * t + 2], stats[:, 6 * t:6 * t + 6])
                    link(ins)
                    dve.tensor_scalar(ret_var[:, 0:4], moments[:, 1:8:2], EPS, None, ALU.add).then_inc(var_set, 1)
                    dve.wait_ge(rstd_set, i + 1)
                    for t in range(TT):
                        b = banks[t // 2][0]
                        ins = dve.tensor_scalar(o_nat[:, t, :], bank[b][:, (t % 2) * VD:(t % 2 + 1) * VD],
                                                moments[:, 2 * t:2 * t + 1], ret_rstd[:, t:t + 1],
                                                ALU.subtract, ALU.mult)
                        if t % 2:
                            ins.then_inc(bank_free[b], 1)
                elif kind == "ret_t":
                    turn_back_head(i, banks)

            chain0 = steps.n
            dve.sem_inc(merged_ready, 1)
            def merge_tile(m, hi_before, first=False):
                if first:
                    split(MERGE0 + AHEAD)
                    turn_back_head(HEADS - 1, banks_of[LAST_TURN])
                for g in range(1 if first else 0, 4):
                    split(MERGE0 + AHEAD + g, 5, m)
                for g in range(N_BRANCHES):
                    if g < 2:
                        dve.wait_ge(blocks_done, 5 * m + MERGE0 + 4 + g)
                    dve.wait_ge(bank_free[g], m + used_merge[g] + 1)
                    dve.tensor_tensor(sig[g][:, :], sig[g][:, :], bank[3 + g][:, :], ALU.mult)\
                        .then_inc(bank_free[3 + g], 1)
                    if g == 0:
                        split(MERGE0 + AHEAD + 4, 5, m)
                for g in (0, 1):
                    dve.wait_ge(bank_free[3 + g], m + used_merge[3 + g] + 1)
                dve.tensor_tensor(sig[0][:, :], sig[0][:, :], sig[1][:, :], ALU.add).then_inc(vec_step, 1)
                dve.wait_ge(vec_step, m + chain0 + 1)
                dve.wait_ge(bank_free[5], m + used_merge[5] + 1)
                dve.tensor_tensor(sig[0][:, :], sig[0][:, :], sig[2][:, :], ALU.add).then_inc(to_round, 1)
                dve.wait_ge(hi_written, m + hi_before + 1)
                dve.tensor_tensor(mrg_lo[:, bass.ds(m, 1), :], sig[0][:, :].rearrange("p (a s) -> p a s", a=1),
                                  r32(mrg_hi[:, bass.ds(m, 1), :]), ALU.subtract).then_inc(merged_ready, 1)

            merge_tile(0, rounded.n + 2, first=True)
            with dve.Fori(1, KD) as m:
                merge_tile(m, rounded.n)
            steps.n += KD
            rounded.n += KD

            def rest_h2(q):
                for c in range(2):
                    k = 2 * q + c
                    rest(h2_lo[:, k, :], bank[X1_BANKS[c]][:, :], h2_hi[:, k, :], gain2[:, k:k + 1])\
                        .then_inc(bank_free[X1_BANKS[c]], 1)

            for q in range(OUT_GROUPS):
                split(OUT0 + 2 * q + AHEAD)
                if q:
                    rest_h2(q - 1)
                four = len(OUT_BANKS[q]) == TT
                for t in range(TT):
                    if q == t == 0:
                        dve.wait_ge(x_in, 16 * TT)
                    if (t if four else t | 1) < TT - 1:
                        dve.wait_ge(out_done, (TT - 1) * q + (t if four else t | 1) + 1)
                    else:
                        dve.wait_ge(blocks_done, OUT0 + 2 * q + 2)
                    b, c0 = OUT_BANKS[q][t if four else t // 2], 0 if four else (t % 2) * OUT_COLS
                    part = x1[:, t, q * OUT_COLS:(q + 1) * OUT_COLS]
                    dve.tensor_tensor(part, bank[b][:, c0:c0 + OUT_COLS], part, ALU.add).then_inc(bank_free[b], 1)
                split(OUT0 + 2 * q + 1 + AHEAD)
            rest_h2(OUT_GROUPS - 1)

            def last_half(t):
                dve.wait_ge(rms_set, MT + TT + t + 1)
                dve.scalar_tensor_tensor(out=y[t][:, S:D], in0=x1[:, t, S:D], scalar=rms[:, t:t + 1],
                                         in1=gain_f[:, S:D], op0=ALU.mult, op1=ALU.mult).then_inc(y_ready[1], 1)

            for half in range(2):
                n0 = FFN0 + half * FFN_HALF_BLOCKS
                pair = FF1_BANKS[half]
                with dve.Fori(0, HALF // 4) as q:
                    for jj in range(4):
                        b = pair[jj % 2]
                        split(n0 + jj + AHEAD, 4, q)
                        dve.wait_ge(bank_free[b], 2 * q + ff1_uses[half][jj % 2] + jj // 2 + 1)
                        dve.tensor_tensor(relu2[jj % 2][:, :], relu[jj % 2][:, :], relu[jj % 2][:, :], ALU.mult)\
                            .then_inc(to_round, 1)
                        dve.wait_ge(hi_written, 4 * q + rounded.n + jj + 1)
                        dve.tensor_tensor(hid_lo[:, bass.ds(4 * q + jj, 1), :],
                                          relu2[jj % 2][:, :].rearrange("p (a s) -> p a s", a=1),
                                          r32(hid_hi[:, bass.ds(4 * q + jj, 1), :]), ALU.subtract)\
                            .then_inc(hid_ready, 1)
                rounded.n += HALF
                for f in range(2):
                    four, uses = FF2_BANKS[half][f], ffn_uses[half][f]
                    for g in range(GROUP):
                        n = n0 + HALF + f * GROUP + g
                        if n + AHEAD < BLOCKS:
                            split(n + AHEAD)
                        if half == f == 1 and g < TT:
                            if g == 0:
                                dve.wait_ge(gain_in, 16)
                            dve.wait_ge(half_sums, g + 1)
                            dve.tensor_tensor(x2g[:, g, :], x1[:, g, 0:S], gain_f[:, 0:S], ALU.mult)
                        if half == f == 1 and g == TT:
                            link(dve.tensor_scalar(half_mean[:, 0:4], ssq[:, 0:4], 1.0 / D, EPS, ALU.mult, ALU.add))
                    if half == f == 0:
                        dve.wait_ge(squares_summed, MT + TT + TT)
                        link(dve.tensor_scalar(msq[:, 0:4], ssq[:, 0:4], 1.0 / D, EPS, ALU.mult, ALU.add))
                        link(dve.reciprocal(inv_ms[:, 0:4], msq[:, 0:4]))
                    if half == 0 or f == 0:
                        dve.wait_ge(blocks_done, n0 + HALF + (f + 1) * GROUP)
                    for t in range(TT):
                        if half == f == 1:
                            dve.wait_ge(tokens_done, t + 1)
                        if half:
                            dve.wait_ge(bank_free[FF2_BANKS[0][f][t]], ffn_uses[0][f][t] + 1)
                        part = x1[:, t, f * S:(f + 1) * S]
                        dve.scalar_tensor_tensor(out=part, in0=bank[four[t]][:, :], scalar=inv_ms[:, t:t + 1],
                                                 in1=part, op0=ALU.mult, op1=ALU.add).then_inc(bank_free[four[t]], 1)
                        if half == f == 1:
                            if t:
                                last_half(t - 1)
                            dve.wait_ge(half_sums, TT + t + 1)
                            dve.scalar_tensor_tensor(out=msq[:, t:t + 1], in0=ssq[:, 4 + t:5 + t], scalar=1.0 / D,
                                                     in1=half_mean[:, t:t + 1], op0=ALU.mult, op1=ALU.add)\
                                .then_inc(msq_set, 1)
            last_half(TT - 1)

        @block.gpsimd
        def _(pool):
            pool.memset(minus_half[:, :], -0.5).then_inc(consts_set, 1)
            pool.memset(ones_row[:, :], 1.0).then_inc(consts_set, 1)
            pool.wait_ge(consts_set, 2)

            def inv_sqrt(dst, src, width):
                return pool.tensor_tensor(dst, src, minus_half[:, 0:width], ALU.pow)

            for s in range(MT + TT):
                pool.wait_ge(msq_set, s + 1)
                inv_sqrt(rms[:, s:s + 1], msq[:, s:s + 1], 1).then_inc(rms_set, 1)
                if s == 1:
                    pool.wait_ge(hi_split, 1)
                    pool.tensor_tensor(w_lo[slots[0]][:, :], w_raw[slots[0]][:, :], r32(w_hi[slots[0]][:, :]),
                                       ALU.subtract).then_inc(lo_split, 1)
            for b, uses in banks_of["turn", MT + 2] + banks_of["turn", MT + 3]:
                pool.wait_ge(bank_free[b], uses + 1)
            for p in padded:
                pool.memset(p[:, :], 0.0).then_inc(pads_set, 1)

            added = 0

            for kind, i, n, banks in STEPS:
                if kind in ("q", "k"):
                    turn = 2 * i + (kind == "k")
                    pool.wait_ge(halves_swapped, turn + 1)
                    if turn:
                        pool.wait_ge(qk_ready, turn)
                    pool.tensor_tensor(work_b[:, :], swapped[:, :], sin[:, :], ALU.mult).then_inc(sin_done, 1)
                elif kind == "pool":
                    b, uses = banks[0]
                    pool.wait_ge(bank_free[b], uses + 1)
                    if i:
                        pool.wait_ge(mixed, i)
                    width = S + 2 * PAD
                    p, dst, src = padded[i % 2], sums[0], sums[1]
                    ins = pool.tensor_tensor(dst[:, 1:width], p[:, 1:width], p[:, 0:width - 1], ALU.add)
                    lo, hi, reach = 1, width, 1
                    for _ in range(i):
                        ins.then_inc(pool_step, 1)
                        added += 1
                        pool.wait_ge(pool_step, added)
                        src, dst = dst, src
                        lo, hi = lo + reach, hi - reach
                        ins = pool.tensor_tensor(dst[:, lo:hi], src[:, lo + reach:hi + reach],
                                                 src[:, lo - reach:hi - reach], ALU.add)
                        reach *= 2
                    ins.then_inc(sums_done, 1)
                elif kind == "ret_v":
                    pool.wait_ge(var_set, i + 1)
                    inv_sqrt(ret_rstd[:, 0:4], ret_var[:, 0:4], 4).then_inc(rstd_set, 1)

            for t in range(TT):
                pool.wait_ge(msq_set, MT + TT + t + 1)
                inv_sqrt(rms[:, t:t + 1], msq[:, t:t + 1], 1).then_inc(rms_set, 1)


_INS = ["x", "mem", "w_in", "ret_decay_logit", "w_ret_o", "w_pool_grp", "pool_scale", "w_pool_o",
        "w_mem_kv", "w_mem_o", "w_out", "w_ff1", "w_ff2", "norm1_g", "norm2_g", "mem_norm_g",
        "final_norm_g"]


def shape_tables():
    f32 = np.float32
    inv = (f32(10000.0) ** (-np.arange(0, P, 2, dtype=f32) / f32(P))).astype(f32)
    angle = (np.arange(S, dtype=f32)[None, :] * inv[:, None]).astype(f32)
    cos, sin = np.cos(angle).astype(f32), np.sin(angle).astype(f32)
    distance = np.arange(SPAN)[None, :] - np.arange(P)[:, None] - REACH
    n = np.arange(S)
    counts = [1.0 / (np.clip(n + w // 2, 0, S) - np.clip(n - w // 2, 0, S)) for w in POOL_WINDOWS]
    return {
        "identity": np.eye(P, dtype=f32),
        "cos_table": np.concatenate([cos, cos]),
        "sin_table": np.concatenate([-sin, sin]),
        "distance": distance.astype(f32),
        "inv_count": np.concatenate(counts)[None, :].astype(f32),
    }


def kernel(**inputs):
    import concourse.bacc as bacc
    from concourse.bass_utils import run_bass_kernel_spmd

    nc = bacc.Bacc("TRN2", target_bir_lowering=False, num_devices=1)
    arrays, args = {}, []
    given = {name: np.ascontiguousarray(inputs[name]) for name in _INS}
    for name, a in {**given, **shape_tables()}.items():
        arrays[f"in_{name}"] = a
        args.append(nc.dram_tensor(f"in_{name}", a.shape, mybir.dt.from_np(a.dtype), kind="ExternalInput").ap())
    out = nc.dram_tensor("out", (1, S, D), FP32, kind="ExternalOutput").ap()
    encoder_kernel(nc, *args, out)
    result = run_bass_kernel_spmd(nc, [arrays], core_ids=[0])
    return result.results[0]["out"]
```
